# Optimizing a Trainium2 kernel written in Bass

```python
import math
import jax
import jax.numpy as jnp
from jax import lax
import numpy as np
import jax, jax.numpy as jnp

D_MODEL = 1024
BATCH = 1
SEQ = 256
DEPTH = 2

N_MIXERS = 3

GDN_DK = 128
GDN_DV = 128
GDN_HEADS = D_MODEL // GDN_DK
GDN_CONV = 4
GDN_CHUNK = 64
GDN_QK = GDN_HEADS * GDN_DK
GDN_V = GDN_HEADS * GDN_DV
GDN_IN = 2 * GDN_QK + 2 * GDN_V + 2 * GDN_HEADS

MOBA_DH = 128
MOBA_HEADS = D_MODEL // MOBA_DH
MOBA_BLOCK = 256
MOBA_TOPK = 3
MOBA_QBLOCK = 16
ROPE_THETA = 500000.0
ROPE_DIMS = MOBA_DH // 4

RET_DK = 256
RET_DV = 512
RET_HEADS = D_MODEL // RET_DK
RET_CHUNK = 128
XPOS_BASE = 10000.0

D_FF = ((8 * D_MODEL + 3 * 256 - 1) // (3 * 256)) * 256

DEEPNORM_ALPHA = (2 * DEPTH) ** 0.25
DEEPNORM_BETA = (8 * DEPTH) ** -0.25
LN_EPS = 1e-5
NORM_EPS = 1e-6
NEG_INF = -1e30
F32 = jnp.float32


def layer_norm(x, g, b):
    xf = x.astype(F32)
    mu = jnp.mean(xf, -1, keepdims=True)
    var = jnp.mean(jnp.square(xf - mu), -1, keepdims=True)
    return ((xf - mu) * lax.rsqrt(var + LN_EPS) * g.astype(F32) + b.astype(F32)).astype(x.dtype)

def split_heads(t, n_heads):
    bsz, seq, width = t.shape
    return t.reshape(bsz, seq, n_heads, width // n_heads).transpose(0, 2, 1, 3)

def l2_normalize(t):
    tf = t.astype(F32)
    return tf * lax.rsqrt(jnp.sum(tf * tf, -1, keepdims=True) + NORM_EPS)

def apply_rotary(x, inv_freq):
    half = inv_freq.shape[0]
    seq = x.shape[2]
    ang = jnp.arange(seq, dtype=F32)[:, None] * inv_freq[None, :]
    cos, sin = jnp.cos(ang), jnp.sin(ang)
    xf = x.astype(F32)
    x1, x2 = xf[..., :half], xf[..., half:2 * half]
    out = jnp.concatenate([x1 * cos - x2 * sin, x1 * sin + x2 * cos, xf[..., 2 * half:]], -1)
    return out.astype(x.dtype)

def causal_depthwise_conv(x, w):
    width, ch = w.shape
    return lax.conv_general_dilated(
        x, w[:, None, :], window_strides=(1,), padding=[(width - 1, 0)],
        dimension_numbers=('NWC', 'WIO', 'NWC'), feature_group_count=ch)

def chunk_gated_delta_rule(q, k, v, g, beta):
    bsz, nh, seq, dk = q.shape
    dv = v.shape[-1]
    c = GDN_CHUNK
    n = seq // c
    q = q.astype(F32).reshape(bsz, nh, n, c, dk)
    k = k.astype(F32).reshape(bsz, nh, n, c, dk)
    v = v.astype(F32).reshape(bsz, nh, n, c, dv)
    gc = jnp.cumsum(g.reshape(bsz, nh, n, c), -1)
    beta = beta.reshape(bsz, nh, n, c)
    tril = jnp.tril(jnp.ones((c, c), bool))
    tril_strict = jnp.tril(jnp.ones((c, c), bool), -1)
    diff = gc[..., :, None] - gc[..., None, :]
    decay = jnp.where(tril, jnp.exp(jnp.where(tril, diff, 0.0)), 0.0)
    k_beta = k * beta[..., None]
    v_beta = v * beta[..., None]
    low = jnp.where(tril_strict, jnp.einsum('bhncd,bhnsd->bhncs', k_beta, k) * decay, 0.0)
    rhs = jnp.concatenate([v_beta, k_beta * jnp.exp(gc)[..., None]], -1)
    sol = lax.linalg.triangular_solve(low, rhs, left_side=True, lower=True, unit_diagonal=True)
    u, w = sol[..., :dv], sol[..., dv:]
    attn_intra = jnp.where(tril, jnp.einsum('bhncd,bhnsd->bhncs', q, k) * decay, 0.0)
    q_dec = q * jnp.exp(gc)[..., None]
    k_dec = k * jnp.exp(gc[..., -1:] - gc)[..., None]
    chunk_decay = jnp.exp(gc[..., -1])

    def step(state, inp):
        u_i, w_i, qd_i, kd_i, a_i, cd_i = inp
        v_new = u_i - w_i @ state
        o_i = qd_i @ state + a_i @ v_new
        state = state * cd_i[..., None, None] + jnp.swapaxes(kd_i, -1, -2) @ v_new
        return state, o_i

    xs = tuple(jnp.moveaxis(t, 2, 0) for t in (u, w, q_dec, k_dec, attn_intra, chunk_decay))
    state0 = jnp.zeros((bsz, nh, dk, dv), F32)
    _, o = lax.scan(step, state0, xs)
    return o.transpose(1, 2, 0, 3, 4).reshape(bsz, nh, seq, dv)

def gated_deltanet(x, w_in, w_conv, a_log, dt_bias, norm_g, w_out):
    bsz, seq, _ = x.shape
    nh = GDN_HEADS
    proj = x @ w_in
    qkv, z, b_logit, a_in = jnp.split(
        proj, [2 * GDN_QK + GDN_V, 2 * GDN_QK + 2 * GDN_V, 2 * GDN_QK + 2 * GDN_V + nh], axis=-1)
    qkv = jax.nn.silu(causal_depthwise_conv(qkv, w_conv))
    q, k, v = jnp.split(qkv, [GDN_QK, 2 * GDN_QK], axis=-1)
    q = l2_normalize(split_heads(q, nh)) * GDN_DK ** -0.5
    k = l2_normalize(split_heads(k, nh))
    v = split_heads(v, nh).astype(F32)
    beta = jax.nn.sigmoid(b_logit.astype(F32)).transpose(0, 2, 1)
    g = -(jnp.exp(a_log.astype(F32)) *
          jax.nn.softplus(a_in.astype(F32) + dt_bias.astype(F32))).transpose(0, 2, 1)
    o = chunk_gated_delta_rule(q, k, v, g, beta).transpose(0, 2, 1, 3)
    o = o * lax.rsqrt(jnp.mean(o * o, -1, keepdims=True) + NORM_EPS) * norm_g.astype(F32)
    o = o * jax.nn.silu(z.astype(F32)).reshape(bsz, seq, nh, GDN_DV)
    return o.reshape(bsz, seq, GDN_V).astype(x.dtype) @ w_out

def moba_attention(x, w_qkv, w_out):
    bsz, seq, _ = x.shape
    nh, dh, bs, qb = MOBA_HEADS, MOBA_DH, MOBA_BLOCK, MOBA_QBLOCK
    q, k, v = jnp.split(x @ w_qkv, 3, axis=-1)
    half = ROPE_DIMS // 2
    inv_freq = jnp.power(ROPE_THETA, -jnp.arange(half, dtype=F32) / half)
    q = apply_rotary(split_heads(q, nh), inv_freq)
    k = apply_rotary(split_heads(k, nh), inv_freq)
    v = split_heads(v, nh)
    nkb = -(-seq // bs)
    pad = nkb * bs - seq
    kp = jnp.pad(k, ((0, 0), (0, 0), (0, pad), (0, 0)))
    vp = jnp.pad(v, ((0, 0), (0, 0), (0, pad), (0, 0)))
    k_blocks = kp.reshape(bsz, nh, nkb, bs, dh)
    v_blocks = vp.reshape(bsz, nh, nkb, bs, dh)
    k_mean = jnp.mean(k_blocks.astype(F32), axis=3)
    topk = min(MOBA_TOPK, nkb)
    scale = dh ** -0.5
    b_idx = jnp.arange(bsz)[:, None, None, None]
    h_idx = jnp.arange(nh)[None, :, None, None]

    def one_query_block(qi):
        q0 = qi * qb
        own = q0 // bs
        q_blk = lax.dynamic_slice_in_dim(q, q0, qb, axis=2).astype(F32)
        gate = jnp.einsum('bhqd,bhnd->bhqn', q_blk, k_mean)
        gate = jnp.where(jnp.arange(nkb) < own, gate, -jnp.inf)
        _, sel = lax.top_k(gate, topk)
        sel_valid = sel < own
        k_sel = k_blocks[b_idx, h_idx, sel].astype(F32)
        v_sel = v_blocks[b_idx, h_idx, sel].astype(F32)
        s_sel = jnp.einsum('bhqd,bhqnkd->bhqnk', q_blk, k_sel) * scale
        s_sel = jnp.where(sel_valid[..., None], s_sel, NEG_INF)
        k_own = lax.dynamic_slice_in_dim(kp, own * bs, bs, axis=2).astype(F32)
        v_own = lax.dynamic_slice_in_dim(vp, own * bs, bs, axis=2).astype(F32)
        s_own = jnp.einsum('bhqd,bhkd->bhqk', q_blk, k_own) * scale
        q_pos = q0 + jnp.arange(qb)
        k_pos = own * bs + jnp.arange(bs)
        s_own = jnp.where(k_pos[None, :] <= q_pos[:, None], s_own, NEG_INF)
        s = jnp.concatenate([s_sel.reshape(bsz, nh, qb, topk * bs), s_own], -1)
        p = jax.nn.softmax(s, axis=-1)
        p_sel = p[..., :topk * bs].reshape(bsz, nh, qb, topk, bs)
        p_own = p[..., topk * bs:]
        return (jnp.einsum('bhqnk,bhqnkd->bhqd', p_sel, v_sel) +
                jnp.einsum('bhqk,bhkd->bhqd', p_own, v_own))

    o = lax.map(one_query_block, jnp.arange(seq // qb))
    o = o.transpose(1, 0, 3, 2, 4).reshape(bsz, seq, nh * dh)
    return o.astype(x.dtype) @ w_out

def chunk_retention(q, k, v, log_gamma):
    bsz, nh, seq, dk = q.shape
    dv = v.shape[-1]
    c = RET_CHUNK
    n = seq // c
    q = q.astype(F32).reshape(bsz, nh, n, c, dk)
    k = k.astype(F32).reshape(bsz, nh, n, c, dk)
    v = v.astype(F32).reshape(bsz, nh, n, c, dv)
    pos = jnp.arange(c, dtype=F32)
    tril = jnp.tril(jnp.ones((c, c), bool))
    rel = jnp.where(tril, pos[:, None] - pos[None, :], 0.0)
    dmat = jnp.where(tril, jnp.exp(log_gamma[:, None, None] * rel), 0.0)
    inner = jnp.einsum('bhncd,bhnsd->bhncs', q, k) * dmat[None, :, None]
    o_inner = jnp.einsum('bhncs,bhnsd->bhncd', inner, v)
    q_dec = q * jnp.exp(log_gamma[:, None] * (pos + 1.0))[None, :, None, :, None]
    k_dec = k * jnp.exp(log_gamma[:, None] * (c - 1.0 - pos))[None, :, None, :, None]
    chunk_decay = jnp.exp(log_gamma * c)[None, :, None, None]

    def step(state, inp):
        qd_i, kd_i, v_i = inp
        out = qd_i @ state
        state = state * chunk_decay + jnp.swapaxes(kd_i, -1, -2) @ v_i
        return state, out

    xs = tuple(jnp.moveaxis(t, 2, 0) for t in (q_dec, k_dec, v))
    state0 = jnp.zeros((bsz, nh, dk, dv), F32)
    _, o_cross = lax.scan(step, state0, xs)
    o = o_inner + o_cross.transpose(1, 2, 0, 3, 4)
    return o.reshape(bsz, nh, seq, dv)

def retention(x, w_in, gn_g, w_out):
    bsz, seq, _ = x.shape
    nh = RET_HEADS
    q, k, v, gate = jnp.split(x @ w_in, [nh * RET_DK, 2 * nh * RET_DK, 2 * nh * RET_DK + nh * RET_DV], axis=-1)
    inv_freq = jnp.power(XPOS_BASE, -jnp.linspace(0.0, 1.0, RET_DK // 2, dtype=F32))
    q = apply_rotary(split_heads(q, nh), inv_freq)
    k = apply_rotary(split_heads(k, nh), inv_freq).astype(F32) * RET_DK ** -0.5
    v = split_heads(v, nh)
    log_gamma = jnp.log1p(-jnp.exp2(-5.0 - jnp.arange(nh, dtype=F32)))
    o = chunk_retention(q, k, v, log_gamma).transpose(0, 2, 1, 3)
    mu = jnp.mean(o, -1, keepdims=True)
    var = jnp.mean(jnp.square(o - mu), -1, keepdims=True)
    o = ((o - mu) * lax.rsqrt(var + LN_EPS)).reshape(bsz, seq, nh * RET_DV) * gn_g.astype(F32)
    o = jax.nn.silu(gate.astype(F32)) * o
    return o.astype(x.dtype) @ w_out

def swiglu(x, w13, w2):
    g, u = jnp.split(x @ w13, 2, axis=-1)
    return (jax.nn.silu(g) * u) @ w2

def first_inputs(seed: int = 0) -> dict:
    key = jax.random.key(seed)
    ks = jax.random.split(key, 24)
    n_a = len(range(0, DEPTH, N_MIXERS))
    n_b = len(range(1, DEPTH, N_MIXERS))
    n_c = len(range(2, DEPTH, N_MIXERS))

    def dense(k, shape, fan_in, gain=1.0):
        return jax.random.normal(k, shape, F32) * (gain * fan_in ** -0.5)

    def gain(k, shape):
        return 1.0 + 0.02 * jax.random.normal(k, shape, F32)

    x = jax.random.normal(ks[0], (BATCH, SEQ, D_MODEL), F32)
    a_w_in = dense(ks[1], (n_a, D_MODEL, GDN_IN), D_MODEL)
    a_conv = dense(ks[2], (n_a, GDN_CONV, 2 * GDN_QK + GDN_V), GDN_CONV)
    a_a_log = jnp.log(jax.random.uniform(ks[3], (n_a, GDN_HEADS), F32, 1.0, 16.0))
    dt = jnp.exp(jax.random.uniform(ks[4], (n_a, GDN_HEADS), F32, math.log(1e-3), math.log(1e-1)))
    a_dt_bias = dt + jnp.log(-jnp.expm1(-dt))
    a_norm_g = gain(ks[5], (n_a, GDN_DV))
    a_w_out = dense(ks[6], (n_a, GDN_V, D_MODEL), GDN_V, DEEPNORM_BETA)
    b_w_qkv = dense(ks[7], (n_b, D_MODEL, 3 * MOBA_HEADS * MOBA_DH), D_MODEL)
    b_w_out = dense(ks[8], (n_b, MOBA_HEADS * MOBA_DH, D_MODEL), MOBA_HEADS * MOBA_DH, DEEPNORM_BETA)
    c_w_in = dense(ks[9], (n_c, D_MODEL, 2 * RET_HEADS * RET_DK + 2 * RET_HEADS * RET_DV), D_MODEL)
    c_gn_g = gain(ks[10], (n_c, RET_HEADS * RET_DV))
    c_w_out = dense(ks[11], (n_c, RET_HEADS * RET_DV, D_MODEL), RET_HEADS * RET_DV, DEEPNORM_BETA)
    f_w13 = dense(ks[12], (DEPTH, D_MODEL, 2 * D_FF), D_MODEL)
    f_w2 = dense(ks[13], (DEPTH, D_FF, D_MODEL), D_FF, DEEPNORM_BETA)
    ln1_g = gain(ks[14], (DEPTH, D_MODEL))
    ln1_b = 0.02 * jax.random.normal(ks[15], (DEPTH, D_MODEL), F32)
    ln2_g = gain(ks[16], (DEPTH, D_MODEL))
    ln2_b = 0.02 * jax.random.normal(ks[17], (DEPTH, D_MODEL), F32)
    return {'x': x, 'a_w_in': a_w_in, 'a_conv': a_conv, 'a_a_log': a_a_log, 'a_dt_bias': a_dt_bias,
            'a_norm_g': a_norm_g, 'a_w_out': a_w_out, 'b_w_qkv': b_w_qkv, 'b_w_out': b_w_out,
            'c_w_in': c_w_in, 'c_gn_g': c_gn_g, 'c_w_out': c_w_out, 'f_w13': f_w13, 'f_w2': f_w2,
            'ln1_g': ln1_g, 'ln1_b': ln1_b, 'ln2_g': ln2_g, 'ln2_b': ln2_b}

def first_block(x, a_w_in, a_conv, a_a_log, a_dt_bias, a_norm_g, a_w_out, b_w_qkv, b_w_out,
              c_w_in, c_gn_g, c_w_out, f_w13, f_w2, ln1_g, ln1_b, ln2_g, ln2_b):
    h = x
    for i in range(DEPTH):
        kind, j = i % N_MIXERS, i // N_MIXERS
        if kind == 0:
            mix = gated_deltanet(h, a_w_in[j], a_conv[j], a_a_log[j], a_dt_bias[j], a_norm_g[j], a_w_out[j])
        elif kind == 1:
            mix = moba_attention(h, b_w_qkv[j], b_w_out[j])
        else:
            mix = retention(h, c_w_in[j], c_gn_g[j], c_w_out[j])
        h = layer_norm(DEEPNORM_ALPHA * h + mix, ln1_g[i], ln1_b[i])
        h = layer_norm(DEEPNORM_ALPHA * h + swiglu(h, f_w13[i], f_w2[i]), ln2_g[i], ln2_b[i])
    return h


DEPTH_2 = 1

GRID_W = 64
CTX_LEN = 256
FF_HALF = 2816
F_GROUPS = 4
F_GROUP_DIM = 128
F_WIDTH = F_GROUPS * F_GROUP_DIM
M_HEADS = 4
M_HEAD_DIM = 256
M_WIDTH = M_HEADS * M_HEAD_DIM
CONV_K = 3
CHUNK = 128
N_ADA = 9
EPS = 1e-6

COL_F = 0
COL_Q = COL_F + F_WIDTH
COL_K = COL_Q + M_WIDTH
COL_V = COL_K + M_WIDTH
COL_O = COL_V + M_WIDTH
COL_GATES = COL_O + M_WIDTH
COL_BR = COL_GATES + 4 * M_HEADS
IN_WIDTH = COL_BR + 2 * D_MODEL


def rmsnorm(x, g):
    xf = x.astype(jnp.float32)
    y = xf * lax.rsqrt(jnp.mean(xf * xf, axis=-1, keepdims=True) + EPS)
    return (y * g.astype(jnp.float32)).astype(x.dtype)

def modulate(x, shift, scale):
    return x * (1 + scale) + shift

def ada_params(cvec, w, b):
    m = jax.nn.silu(cvec) @ w + b
    return m.reshape(cvec.shape[0], N_ADA, 1, D_MODEL)

def swiglu_2(u, w13, w2):
    a, b = jnp.split(u @ w13, 2, axis=-1)
    return (jax.nn.silu(a) * b) @ w2

def half_ffn(h, shift, scale, gate, g_pre, g_post, w13, w2):
    u = modulate(rmsnorm(h, g_pre), shift, scale)
    return h + 0.5 * gate * rmsnorm(swiglu_2(u, w13, w2), g_post)

def dwconv(x, w, b):
    y = lax.conv_general_dilated(
        x, w[:, None, :].astype(x.dtype), window_strides=(1,),
        padding=[(CONV_K // 2, CONV_K // 2)],
        dimension_numbers=("NWC", "WIO", "NWC"),
        feature_group_count=x.shape[-1])
    return y + b

def to_heads(x):
    B, T, _ = x.shape
    return x.reshape(B, T, M_HEADS, M_HEAD_DIM).transpose(0, 2, 1, 3)

def fourier_latent(xf):
    B, T, _ = xf.shape
    rows = T // GRID_W
    z = xf.astype(jnp.float32).reshape(B, rows, GRID_W, F_GROUPS, F_GROUP_DIM)
    y = jnp.fft.fftn(z, axes=(1, 2, 4), norm="ortho").real
    return y.reshape(B, T, F_WIDTH).astype(xf.dtype)

def fourier_context(xf):
    B, T, _ = xf.shape
    z = xf.astype(jnp.float32).reshape(B, T, F_GROUPS, F_GROUP_DIM)
    y = jnp.fft.fftn(z, axes=(1, 3), norm="ortho").real
    return y.reshape(B, T, F_WIDTH).astype(xf.dtype)

def project(u, w_in, b_in, conv_w, conv_b):
    B, T, _ = u.shape
    p = u @ w_in + b_in
    xf = p[..., COL_F:COL_Q]
    qk = jax.nn.silu(dwconv(p[..., COL_Q:COL_V], conv_w, conv_b))
    q = to_heads(qk[..., :M_WIDTH])
    k = to_heads(qk[..., M_WIDTH:])
    v = to_heads(p[..., COL_V:COL_O])
    o = p[..., COL_O:COL_GATES]
    gates = p[..., COL_GATES:COL_BR].astype(jnp.float32)
    gates = gates.reshape(B, T, 4, M_HEADS).transpose(2, 0, 3, 1)
    gate_pre = (gates[0], jax.nn.log_sigmoid(gates[1]), gates[2], jax.nn.log_sigmoid(gates[3]))
    g_f = p[..., COL_BR:COL_BR + D_MODEL]
    g_m = p[..., COL_BR + D_MODEL:]
    return xf, q, k, v, o, gate_pre, g_f, g_m

def mlstm_scan(q, k, v, li, lf, state):
    B, H, T, DK = q.shape
    NC = T // CHUNK

    def chunks(a):
        a = a.astype(jnp.float32).reshape(B, H, NC, CHUNK, *a.shape[3:])
        return jnp.moveaxis(a, 2, 0)

    qc, kc, vc, lic, lfc = map(chunks, (q, k * (DK ** -0.5), v, li, lf))
    lower = jnp.tril(jnp.ones((CHUNK, CHUNK), dtype=bool))

    def step(carry, inp):
        C, n, m = carry
        qx, kx, vx, lix, lfx = inp
        b = jnp.cumsum(lfx, axis=-1)
        dmat = b[..., :, None] - b[..., None, :] + lix[..., None, :]
        dmat = jnp.where(lower, dmat, -jnp.inf)
        inter = b + m[..., None]
        m_t = jnp.maximum(inter, jnp.max(dmat, axis=-1))
        w = jnp.exp(dmat - m_t[..., None])
        a = jnp.exp(inter - m_t)
        s = jnp.einsum("bhtd,bhsd->bhts", qx, kx) * w
        num = a[..., None] * jnp.einsum("bhtd,bhde->bhte", qx, C) + jnp.einsum("bhts,bhse->bhte", s, vx)
        den = a * jnp.einsum("bhtd,bhd->bht", qx, n) + jnp.sum(s, axis=-1)
        h = num / jnp.maximum(jnp.abs(den), jnp.exp(-m_t))[..., None]
        bL = b[..., -1]
        g = bL[..., None] - b + lix
        m_new = jnp.maximum(bL + m, jnp.max(g, axis=-1))
        decay = jnp.exp(bL + m - m_new)
        wk = jnp.exp(g - m_new[..., None])
        C_new = decay[..., None, None] * C + jnp.einsum("bhsd,bhse->bhde", kx * wk[..., None], vx)
        n_new = decay[..., None] * n + jnp.einsum("bhs,bhsd->bhd", wk, kx)
        return (C_new, n_new, m_new), h

    state_out, hs = lax.scan(step, state, (qc, kc, vc, lic, lfc))
    h = jnp.moveaxis(hs, 0, 2).reshape(B, H, T, -1)
    return h.astype(q.dtype), state_out

def bidir_mlstm(q, k, v, gate_pre, state_f, state_b):
    li_f, lf_f, li_b, lf_b = gate_pre
    h_f, s_f = mlstm_scan(q, k, v, li_f, lf_f, state_f)
    flip = lambda a: jnp.flip(a, axis=2)
    h_b, s_b = mlstm_scan(flip(q), flip(k), flip(v), flip(li_b), flip(lf_b), state_b)
    return h_f + flip(h_b), s_f, s_b

def merge(y_fourier, h, o, g_f, g_m, head_g, w_four, w_mproj, w_out):
    B, H, T, dh = h.shape
    hn = rmsnorm(h.transpose(0, 2, 1, 3), head_g.reshape(M_HEADS, M_HEAD_DIM)).reshape(B, T, M_WIDTH)
    hm = jax.nn.sigmoid(o) * hn
    y = jax.nn.sigmoid(g_f) * (y_fourier @ w_four) + jax.nn.sigmoid(g_m) * (hm @ w_mproj)
    return y @ w_out

def token_mixing(h_lat, h_ctx, mod_l, mod_c, g_pre, g_post, w_in, b_in, conv_w, conv_b,
                 head_g, w_four, w_mproj, w_out, update_ctx):
    sh_l, sc_l, gt_l = mod_l
    sh_c, sc_c, gt_c = mod_c
    pl = project(modulate(rmsnorm(h_lat, g_pre), sh_l, sc_l), w_in, b_in, conv_w, conv_b)
    pc = project(modulate(rmsnorm(h_ctx, g_pre), sh_c, sc_c), w_in, b_in, conv_w, conv_b)
    B = h_ctx.shape[0]
    zero = (jnp.zeros((B, M_HEADS, M_HEAD_DIM, M_HEAD_DIM), jnp.float32),
            jnp.zeros((B, M_HEADS, M_HEAD_DIM), jnp.float32),
            jnp.zeros((B, M_HEADS), jnp.float32))
    h_c, s_f, s_b = bidir_mlstm(pc[1], pc[2], pc[3], pc[5], zero, zero)
    h_l, _, _ = bidir_mlstm(pl[1], pl[2], pl[3], pl[5], s_f, s_b)
    out_l = merge(fourier_latent(pl[0]), h_l, pl[4], pl[6], pl[7], head_g, w_four, w_mproj, w_out)
    new_lat = h_lat + gt_l * rmsnorm(out_l, g_post)
    new_ctx = None
    if update_ctx:
        out_c = merge(fourier_context(pc[0]), h_c, pc[4], pc[6], pc[7], head_g, w_four, w_mproj, w_out)
        new_ctx = h_ctx + gt_c * rmsnorm(out_c, g_post)
    return new_lat, new_ctx

def second_inputs(seed: int = 0) -> dict:
    key = jax.random.key(seed)
    ks = jax.random.split(key, 20)
    nrm = lambda k, shape, s: jax.random.normal(k, shape, jnp.float32) * s
    D = D_MODEL
    b_in = nrm(ks[10], (DEPTH_2, IN_WIDTH), 0.02)
    f_bias = jnp.linspace(3.0, 6.0, M_HEADS, dtype=jnp.float32)
    b_in = b_in.at[:, COL_GATES + M_HEADS:COL_GATES + 2 * M_HEADS].add(f_bias)
    b_in = b_in.at[:, COL_GATES + 3 * M_HEADS:COL_GATES + 4 * M_HEADS].add(f_bias)
    return {
        "x": nrm(ks[0], (BATCH, SEQ, D), 1.0),
        "c": nrm(ks[1], (BATCH, D), 1.0),
        "ctx": nrm(ks[2], (BATCH, CTX_LEN, D), 1.0),
        "c_ctx": nrm(ks[3], (D,), 1.0),
        "w_ada": nrm(ks[4], (DEPTH_2, D, N_ADA * D), D ** -0.5),
        "b_ada": nrm(ks[5], (DEPTH_2, N_ADA * D), 0.02),
        "norm_g": 1.0 + nrm(ks[6], (DEPTH_2, 6, D), 0.05),
        "w13_a": nrm(ks[7], (DEPTH_2, D, 2 * FF_HALF), D ** -0.5),
        "w2_a": nrm(ks[8], (DEPTH_2, FF_HALF, D), FF_HALF ** -0.5),
        "w_in": nrm(ks[9], (DEPTH_2, D, IN_WIDTH), D ** -0.5),
        "b_in": b_in,
        "conv_w": nrm(ks[11], (DEPTH_2, CONV_K, 2 * M_WIDTH), CONV_K ** -0.5),
        "conv_b": nrm(ks[12], (DEPTH_2, 2 * M_WIDTH), 0.02),
        "head_g": 1.0 + nrm(ks[13], (DEPTH_2, M_WIDTH), 0.05),
        "w_four": nrm(ks[14], (DEPTH_2, F_WIDTH, D), F_WIDTH ** -0.5),
        "w_mproj": nrm(ks[15], (DEPTH_2, M_WIDTH, D), M_WIDTH ** -0.5),
        "w_out": nrm(ks[16], (DEPTH_2, D, D), D ** -0.5),
        "w13_b": nrm(ks[17], (DEPTH_2, D, 2 * FF_HALF), D ** -0.5),
        "w2_b": nrm(ks[18], (DEPTH_2, FF_HALF, D), FF_HALF ** -0.5),
    }

def second_block(x, c, ctx, c_ctx, w_ada, b_ada, norm_g, w13_a, w2_a, w_in, b_in, conv_w, conv_b,
              head_g, w_four, w_mproj, w_out, w13_b, w2_b):
    h_lat = x
    h_ctx = ctx
    for l in range(DEPTH_2):
        last = l == DEPTH_2 - 1
        ml = ada_params(c, w_ada[l], b_ada[l])
        mc = ada_params(c_ctx[None], w_ada[l], b_ada[l])
        g = norm_g[l]
        h_lat = half_ffn(h_lat, ml[:, 0], ml[:, 1], ml[:, 2], g[0], g[1], w13_a[l], w2_a[l])
        h_ctx = half_ffn(h_ctx, mc[:, 0], mc[:, 1], mc[:, 2], g[0], g[1], w13_a[l], w2_a[l])
        h_lat, h_ctx_new = token_mixing(
            h_lat, h_ctx, (ml[:, 3], ml[:, 4], ml[:, 5]), (mc[:, 3], mc[:, 4], mc[:, 5]),
            g[2], g[3], w_in[l], b_in[l], conv_w[l], conv_b[l], head_g[l],
            w_four[l], w_mproj[l], w_out[l], not last)
        h_lat = half_ffn(h_lat, ml[:, 6], ml[:, 7], ml[:, 8], g[4], g[5], w13_b[l], w2_b[l])
        if not last:
            h_ctx = half_ffn(h_ctx_new, mc[:, 6], mc[:, 7], mc[:, 8], g[4], g[5], w13_b[l], w2_b[l])
    return h_lat


def setup_inputs(seed=0):
    out = dict(first_inputs(seed))
    for name, value in second_inputs(seed + 1).items():
        if name != "x":
            out[name + "_2"] = value
    return out


def reference(
    x, a_w_in, a_conv, a_a_log, a_dt_bias, a_norm_g, a_w_out, b_w_qkv, b_w_out, c_w_in, c_gn_g,
    c_w_out, f_w13, f_w2, ln1_g, ln1_b, ln2_g, ln2_b, c_2, ctx_2, c_ctx_2, w_ada_2, b_ada_2,
    norm_g_2, w13_a_2, w2_a_2, w_in_2, b_in_2, conv_w_2, conv_b_2, head_g_2, w_four_2,
    w_mproj_2, w_out_2, w13_b_2, w2_b_2,
):
    x = first_block(
        x, a_w_in, a_conv, a_a_log, a_dt_bias, a_norm_g, a_w_out, b_w_qkv, b_w_out, c_w_in,
        c_gn_g, c_w_out, f_w13, f_w2, ln1_g, ln1_b, ln2_g, ln2_b,
    )
    return second_block(
        x, c_2, ctx_2, c_ctx_2, w_ada_2, b_ada_2, norm_g_2, w13_a_2, w2_a_2, w_in_2, b_in_2,
        conv_w_2, conv_b_2, head_g_2, w_four_2, w_mproj_2, w_out_2, w13_b_2, w2_b_2,
    )


_drawn_inputs = setup_inputs


def setup_inputs(seed=0):
    import zlib

    import numpy as np

    out = dict(_drawn_inputs(seed))
    spreads = {}
    factors = {'a_norm_g': 21.558, 'conv_b_2': 40.029, 'head_g_2': 4.151}
    for name, (base, spread) in spreads.items():
        noise = np.random.default_rng([zlib.crc32(name.encode()), seed]).standard_normal(out[name].shape)
        drawn = base * np.exp(spread * noise) if base else spread * noise
        out[name] = jnp.asarray(drawn.astype(out[name].dtype))
    for name, factor in factors.items():
        out[name] = (out[name] * factor).astype(out[name].dtype)
    return out
```

```python
from contextlib import ExitStack

import numpy as np

import concourse.bass as bass
from concourse import mybir

F32 = mybir.dt.float32
F32R = mybir.dt.float32r
ALU = mybir.AluOpType
ACT = mybir.ActivationFunctionType
AX = mybir.AxisListType.X

P = 128
T = 256
TT = T // P
D = 1024
KD = D // P
FF = 2816
KF = FF // P
ALPHA = 4 ** 0.25
LN_EPS = 1e-5
EPS = 1e-6

CC = 256
CHUNK = KD * CC
RING = 3

G_HEADS = 8
G_CHUNK = 64
M_HEADS = 4
MD = 256
NEG = -1e30
N_SMALL = 740
ARENA = 78

TAKES_OVER = {
    "ada_ps": ("diag", 8), "silu_c": ("normed", 8),
    "ada_row": ("diag_g", 4), "ada_cols": ("diag_b", 4), "ada": ("row_ps", 4),
    "mods": ("rowb_ps", 4), "gate_diag": ("erow", 4), "gate_row": ("dt_diff", 4),
    "gate_ps": ("qk_ps", 4), "res_scaled": ("ktok", 4), "res_sq": ("vbeta", 4),
    "res_a": ("kv_ps", 4), "res_rn": ("lowt", 4), "res": ("low0", 4), "rms_sq": ("low1", 4),
    "rms_mean": ("att", 4), "rms_rn": ("inv0", 4), "taps3": ("inv0_ps", 4), "conv3": ("invcopy", 4),
    "m_gate": ("clev0", 4), "m_soft": ("w_ps", 20), "m_log": ("wlev", 20),
    "m_exp": ("twt_ps", 20), "m_rows_ps": ("invup", 16), "m_rows": ("invtup", 20),
    "m_first": ("kbg", 4), "m_next": ("kd", 4), "m_scan": ("uw", 8), "m_nlast": ("uw_ps", 4),
    "m_ddiff": ("v_ps", 8), "m_mt": ("vnew", 8), "m_dec": ("o_ps", 8), "m_dd": ("o", 8),
    "m_cols_ps": ("s_ps", 8), "m_cols": ("st", 8), "m_cols0": ("st_dec", 8), "m_wk": ("qdec", 4),
    "m_a": ("cdk", 4), "m_em": ("onorm", 2), "k_tok": ("ot_ps", 4), "k_tok_ps": ("gated", 4),
    "cell": ("g_hi", 4), "kw": ("g_lo", 4), "ones_col": ("dt", 4), "cell_ps": ("dt_m1", 4),
    "w_diff": ("dt_exp", 4), "s_t": ("osq", 2), "cm_ps": ("osum", 2), "hden": ("orn", 2),
    "nq": ("omean", 2), "hneg": ("squares", 8),
    "sig_first": ("rotated", 8), "hsq": ("roped", 4), "hss": ("qkt_ps", 8), "hmean": ("qkt", 8),
    "h_rn": ("scores", 8), "sig_og": ("probs0", 8), "hnorm": ("probs", 8), "zf_ps": ("pt_ps", 8),
    "zf": ("pt", 8), "yf_ps": ("att_o", 8), "yf": ("exps", 16), "yf_lo": ("maxes", 16),
    "hm_ps": ("inv_sum", 8), "hm": ("row_max", 8), "hm_hi": ("scored", 8), "hm_lo": ("o_copy", 8),
    "y_sum": ("o_hi", 8), "y_hi": ("o_lo", 8), "y_lo": ("norm_rows", 8),
}

COL_F, COL_Q, COL_K, COL_V, COL_O, COL_GATES = 0, 512, 1536, 2560, 3584, 4608
COL_BR = COL_GATES + 4 * M_HEADS

TABLES = {}


def _add_table(name, width):
    TABLES[name] = (sum(w for _, w in TABLES.values()), width)


for _name, _width in [("ident", 128), ("ones", 128), ("u64", 128), ("us64", 128), ("blk64", 128),
                      ("level", 6 * 128), ("uf", 128), ("ub", 128), ("causal", 384),
                      ("rope", 64), ("sel", 4 * 128), ("cd", 128), ("nsd", 128)]:
    _add_table(_name, _width)
N_TABLE = sum(w for _, w in TABLES.values())


def shape_tables():
    i = np.arange(P)
    same = (i[:, None] // G_CHUNK) == (i[None, :] // G_CHUNK)
    t = {
        "ident": np.eye(P), "ones": np.ones((P, P)),
        "u64": same & (i[:, None] <= i[None, :]), "us64": same & (i[:, None] < i[None, :]),
        "blk64": same, "uf": i[:, None] <= i[None, :], "ub": i[:, None] >= i[None, :],
    }
    t["level"] = np.concatenate(
        [((i[:, None] >> (s + 1)) == (i[None, :] >> (s + 1))) & ((i[:, None] >> s) % 2 == 0)
         & ((i[None, :] >> s) % 2 == 1) for s in range(6)], 1)
    future = np.where(i[None, :] > i[:, None], NEG, 0.0)
    t["causal"] = np.concatenate([future, np.zeros((P, P)), future], 1)
    half = 16
    inv = np.power(np.float32(500000.0), -np.arange(half, dtype=np.float32) / np.float32(half))
    ang = (np.arange(T, dtype=np.float32)[:, None] * inv[None, :]).astype(np.float32)
    rope = np.stack([np.cos(ang), np.sin(ang)], 1).reshape(TT, P, 2, half)
    t["rope"] = rope.transpose(1, 0, 2, 3).reshape(P, 64)
    sel = np.zeros((P, 4, P))
    for h in range(4):
        sel[h, h] = 1
    t["sel"] = sel.reshape(P, 4 * P)
    th = 2 * np.pi * (i[:, None] * i[None, :] % P) / P
    t["cd"], t["nsd"] = np.cos(th) / np.sqrt(P), -np.sin(th) / np.sqrt(P)
    table = np.zeros((P, N_TABLE), np.float32)
    for name, (at, width) in TABLES.items():
        table[:, at:at + width] = t[name]
    r, c = np.arange(T) // 64, np.arange(T) % 64
    th = 2 * np.pi * (r[:, None] * r[None, :] % 4 / 4 + c[:, None] * c[None, :] % 64 / 64)
    tok = np.stack([np.cos(th), np.sin(th)], 0) / np.sqrt(T)
    tok = tok.reshape(2, TT, P, T).transpose(2, 0, 1, 3).reshape(P, 2 * TT * T).astype(np.float32)
    return table, tok


class Segment:

    def __init__(self, name, n, kind, src, k=KD):
        self.name, self.n, self.kind, self.src, self.k = name, n, kind, src, k
        self.first = self.out = 0
        self.last = False


def walk(eng, seg, body):
    body_static = min(RING, seg.n)
    for j in range(body_static):
        c = seg.first + j
        body(j, c % RING, c // RING)
    turns = ((seg.n - RING if seg.last else seg.n) - RING) // RING
    start = body_static
    if turns >= 2:
        with eng.Fori(0, turns) as i:
            for u in range(RING):
                c = seg.first + RING + u
                body(i * RING + (RING + u), c % RING, i + c // RING)
        start += turns * RING
    for j in range(start, seg.n):
        c = seg.first + j
        body(j, c % RING, c // RING)


def wait_from(eng, sem, value):
    if not isinstance(value, int) or value > 0:
        eng.wait_ge(sem, value)


def build(nc, A, out):
    ctx = ExitStack()
    SLOT = CHUNK * 4

    def sb(name, shape, dt=F32):
        return ctx.enter_context(nc.sbuf_tensor(name, shape, dt))

    raw = sb("raw", [P, RING, CHUNK])
    whi = sb("whi", [P, RING, CHUNK], F32R)
    wlo = sb("wlo", [P, RING, CHUNK], F32R)
    ah = sb("ah", [P, KD, T], F32R)
    al = sb("al", [P, KD, T], F32R)
    x0 = sb("x0", [P, TT, D])
    x1 = sb("x1", [P, TT, D])
    gb = sb("gb", [P, 2, D])
    table = sb("table", [P, N_TABLE])
    cols = sb("cols", [P, 4, P])
    adat = sb("adat", [P, 144])
    small = sb("small", [P, N_SMALL])
    swh = sb("swh", [P, KD, 16], F32R)
    swl = sb("swl", [P, KD, 16], F32R)
    base = -(-nc.sbuf_base // 64) * 64
    assert base + ARENA * 1024 <= nc.sbuf_usable_end, (base, nc.sbuf_usable_end)

    def at(name, kb, shape, dt=F32):
        size = int(np.prod(shape[1:])) * 4
        assert kb * 1024 + size <= ARENA * 1024, name
        return nc.alloc_sbuf_tensor_at(name, shape, dt, offset=base + int(kb * 1024))

    g_raw = at("g_raw", 51, [P, KD, 16])

    def tab(name, *dims):
        off, width = TABLES[name]
        ap = table[:, off:off + width]
        return ap.rearrange("p (a b) -> p a b", a=dims[0]) if dims else ap

    xn = at("xn", 66, [P, TT, D])
    tadd = at("tadd", 74, [P, 2, 512])

    ps = [ctx.enter_context(nc.psum_tensor(f"ps{n}", [P, 512], F32)) for n in range(8)]

    def bank(n, a):
        return ps[n][:, :].rearrange("p (a b) -> p a b", a=a)

    used = [0]

    def sm(width):
        a = small[:, used[0]:used[0] + width]
        used[0] += width
        assert used[0] <= N_SMALL
        return a

    sems = {}

    def S(name, value=None):
        old, ended = TAKES_OVER.get(name, (name, 0))
        if old not in sems:
            sems[old] = ctx.enter_context(nc.semaphore(old))
        return sems[old] if value is None else (sems[old], value + ended)

    def columns(w, off=0):
        v = w.rearrange("(k p) n -> p k n", p=P)

        def src(j, slot):
            dst = raw[:, slot, :].rearrange("p (k n) -> p k n", k=KD)
            for h in range(2):
                yield dst[:, 4 * h:4 * h + 4, :], v[:, 4 * h:4 * h + 4, bass.ds(j * CC + off, CC)]
        return src

    def gate_up(w):
        v = w.rearrange("(k p) n -> p k n", p=P)

        def src(j, slot):
            dst = raw[:, slot, :].rearrange("p (k h n) -> p k h n", k=KD, h=2)
            for h in range(2):
                yield dst[:, :, h, :], v[:, :, bass.ds(j * P + h * FF, P)]
        return src

    def rows(w):
        v = w.rearrange("(k p) n -> p k n", p=P)

        def src(j, slot):
            dst = raw[:, slot, :].rearrange("p (k n) -> p k n", k=2)
            for h in range(2):
                yield dst[:, h:h + 1, :], v[:, bass.ds(j * 2 + h, 1), :]
        return src

    def columns4(w):
        v = w.rearrange("(k p) n -> p k n", p=P)

        def src(j, slot):
            dst = raw[:, slot, 0:4 * CC].rearrange("p (k n) -> p k n", k=4)
            for h in range(2):
                yield dst[:, 2 * h:2 * h + 2, :], v[:, 2 * h:2 * h + 2, bass.ds(j * CC, CC)]
        return src

    w_in = A["w_in_2"][0]
    segs = {}
    order = [
        Segment("g_qkv", 12, "B", columns(A["a_w_in"][0])),
        Segment("g_z", 4, "B", columns(A["a_w_in"][0], 3072)),
        Segment("g_out", 4, "A", columns(A["a_w_out"][0])),
        Segment("up0", KF, "B", gate_up(A["f_w13"][0])),
        Segment("down0", KF // 2, "W2", rows(A["f_w2"][0])),
        Segment("m_qkv", 12, "A", columns(A["b_w_qkv"][0])),
        Segment("m_out", 4, "A", columns(A["b_w_out"][0])),
        Segment("up1", KF, "B", gate_up(A["f_w13"][1])),
        Segment("down1", KF // 2, "W2", rows(A["f_w2"][1])),
        Segment("up2", KF, "B", gate_up(A["w13_a_2"][0])),
        Segment("down2", KF // 2, "W2", rows(A["w2_a_2"][0])),
        Segment("c_k", 4, "B", columns(w_in, COL_K)),
        Segment("c_v", 4, "A", columns(w_in, COL_V)),
        Segment("up3", KF, "B", gate_up(A["w13_a_2"][0])),
        Segment("down3", KF // 2, "W2", rows(A["w2_a_2"][0])),
        Segment("l_k", 4, "B", columns(w_in, COL_K)),
        Segment("l_v", 4, "A", columns(w_in, COL_V)),
        Segment("l_q", 4, "B", columns(w_in, COL_Q)),
        Segment("l_f", 2, "B", columns(w_in, COL_F)),
        Segment("l_o", 4, "B", columns(w_in, COL_O)),
        Segment("l_br", 8, "B", columns(w_in, COL_BR)),
        Segment("four", 4, "B", columns4(A["w_four_2"][0]), k=4),
        Segment("mproj", 4, "B", columns(A["w_mproj_2"][0])),
        Segment("w_out", 4, "A", columns(A["w_out_2"][0])),
        Segment("up4", KF, "B", gate_up(A["w13_b_2"][0])),
        Segment("down4", KF // 2, "W2", rows(A["w2_b_2"][0])),
    ]
    first = 0
    count = {"taken": 0, "hid": 0}
    for q in order:
        q.sem = "hid" if q.name.startswith("up") else "taken"
        q.first, q.before = first, dict(count)
        first += q.n
        if q.kind != "W2":
            count[q.sem] += q.n
        segs[q.name] = q
    order[-1].last = True
    TOTAL = first

    def load_stream(sp):
        for q in order:
            def load(j, slot, turn, q=q):
                wait_from(sp, *S("lo_ready", turn * RING + slot - RING + 1))
                for dst, src in q.src(j, slot):
                    sp.dma_start(dst, src).then_inc(S(f"landed{slot}"), 16)
            walk(sp, q, load)

    def cut_hi(act, slot, turn):
        act.wait_ge(*S(f"landed{slot}", turn * 32 + 32))
        wait_from(act, *S("used", turn * RING + slot - RING + 1))
        act.copy(whi[:, slot, :], raw[:, slot, :]).then_inc(S("hi_ready"), 1)

    def cut_lo(dve, slot, turn):
        dve.wait_ge(*S("hi_ready", turn * RING + slot + 1))
        dve.tensor_tensor(wlo[:, slot, :], raw[:, slot, :], whi[:, slot, :].bitcast(F32),
                          ALU.subtract).then_inc(S("lo_ready"), 1)

    def cut_ahead(eng, q, j, slot, turn):
        if q.last and isinstance(j, int) and j + RING >= q.n:
            return
        if eng is nc.scalar:
            cut_hi(eng, slot, turn + 1)
        else:
            cut_lo(eng, slot, turn + 1)

    def start_cuts(eng):
        for slot in range(RING):
            if eng is nc.scalar:
                cut_hi(eng, slot, 0)
            else:
                cut_lo(eng, slot, 0)

    def products(pe, out_ap, pairs):
        last = None
        n = len(pairs)
        for i, (a, b) in enumerate(pairs):
            last = pe.matmul(out_ap, a, b, start=(i == 0), stop=(i == n - 1))
        return last

    def stream_pe(pe, name, xh, xl):
        q = segs[name]

        def body(j, slot, turn):
            pe.wait_ge(*S("lo_ready", turn * RING + slot + 1))
            if q.kind == "W2":
                w = [p[:, slot, :].rearrange("p (k n) -> p k n", k=2) for p in (whi, wlo)]
                for kk in range(2):
                    k = 2 * j + kk
                    for tt in range(TT):
                        c = slice(tt * P, tt * P + P)
                        for h in range(2):
                            n = slice(512 * h, 512 * h + 512)
                            for i, (x, y) in enumerate([(xh, w[0]), (xh, w[1]), (xl, w[0])]):
                                last = pe.matmul(ps[4 + 2 * tt + h][:, :], x[:, k, c], y[:, kk, n],
                                                 start=(k == 0 and i == 0),
                                                 stop=(k == KF - 1 and i == 2))
                last.then_inc(S("used"), 1)
                return
            if isinstance(j, int) and j < RING:
                for name_, value in q.before.items():
                    wait_from(pe, *S(name_, value))
            else:
                pe.wait_ge(*S(q.sem, j + (q.before[q.sem] - RING + 1)))
            wh = whi[:, slot, 0:q.k * CC].rearrange("p (k n) -> p k n", k=q.k)
            wl = wlo[:, slot, 0:q.k * CC].rearrange("p (k n) -> p k n", k=q.k)
            for f in range(2):
                pairs = []
                for k in range(q.k):
                    if q.kind == "B":
                        c = slice(f * P, f * P + P)
                        pairs += [(wh[:, k, c], xh[:, k, :]), (wh[:, k, c], xl[:, k, :]),
                                  (wl[:, k, c], xh[:, k, :])]
                    else:
                        c = slice(f * P, f * P + P)
                        pairs += [(xh[:, k, c], wh[:, k, :]), (xh[:, k, c], wl[:, k, :]),
                                  (xl[:, k, c], wh[:, k, :])]
                last = products(pe, ps[slot][:, f * CC:f * CC + CC], pairs)
            last.then_inc(S("used"), 1)

        if q.kind == "W2":
            for j in range(q.n):
                c = q.first + j
                body(j, c % RING, c // RING)
        else:
            walk(pe, q, body)

    ident, ones = tab("ident"), tab("ones")
    eps_col = sm(1)
    half_neg = sm(32)
    a_log, dt_bias = sm(8), sm(8)
    gate_bias = sm(16)
    two = lambda v, n: v.rearrange("(r c) -> r c", c=P)[0:n]
    b_in = A["b_in_2"][0]
    groups = [
        [("a_conv", A["a_conv"][0].rearrange("j (r c) -> (j r) c", c=P), 96),
         ("a_norm", A["a_norm_g"], 1), ("conv_b", two(A["conv_b_2"][0], 16), 16)],
        [("b_ada", two(A["b_ada_2"][0], 72), 72),
         ("norm_g", A["norm_g_2"][0].rearrange("j (r c) -> (j r) c", c=P), 48)],
        [("conv_w", A["conv_w_2"][0].rearrange("j (r c) -> (j r) c", c=P), 48),
         ("head_g", two(A["head_g_2"][0], 8), 8), ("c", two(A["c_2"][0], 8), 8),
         ("c_ctx", two(A["c_ctx_2"], 8), 8),
         ("ln1_g", A["ln1_g"].rearrange("j (r c) -> (j r) c", c=P), 16),
         ("ln1_b", A["ln1_b"].rearrange("j (r c) -> (j r) c", c=P), 16)],
        [("ln2_g", A["ln2_g"].rearrange("j (r c) -> (j r) c", c=P), 16),
         ("ln2_b", A["ln2_b"].rearrange("j (r c) -> (j r) c", c=P), 16),
         ("b_in", two(b_in[0:COL_GATES], 36), 36),
         ("b_br", two(b_in[COL_BR:COL_BR + 2 * D], 16), 16)],
    ]
    where = {}
    prow = at("prow", 0, [P, 4, P])
    for g, members in enumerate(groups):
        r = 0
        for name, _, n in members:
            where[name] = (g, r, n)
            r += n
    GROUP_ROWS = [sum(n for _, _, n in m) for m in groups]

    def col(name, i=0, n=1):
        g, r, _ = where[name]
        return cols[:, g, bass.ds(i + r, n)]

    def load_params(act):
        act.dma_start(table[:, :], A["table"]).then_inc(S("tables_in"), 16)
        act.dma_start(x0[:, :, :], A["x"][0].rearrange("(t p) d -> p t d", p=P)).then_inc(S("x_in"), 16)
        for g, members in enumerate(groups):
            for name, src, n in members:
                r = where[name][1]
                act.dma_start(prow[r:r + n, g, :], src).then_inc(S("params_in"), 16)
        act.dma_start(a_log, A["a_a_log"].broadcast_to([P, 8])).then_inc(S("params_in"), 16)
        act.dma_start(dt_bias, A["a_dt_bias"].broadcast_to([P, 8])).then_inc(S("params_in"), 16)
        act.dma_start(gate_bias, A["b_in_2"][:, COL_GATES:COL_BR].broadcast_to([P, 16]))\
           .then_inc(S("params_in"), 16)
    N_PARAM_DMA = sum(len(m) for m in groups) + 3

    def setup_pool(pool):
        pool.memset(half_neg, -0.5).then_inc(S("powers"), 1)

    def params_pe(pe):
        pe.wait_ge(*S("tables_in", 16))
        pe.wait_ge(*S("params_in", 16 * N_PARAM_DMA))
        for g in range(4):
            n = GROUP_ROWS[g]
            last = pe.transpose(ps[3][:, g * P:g * P + n], prow[0:n, g, :], ident[0:n, 0:n])
        last.then_inc(S("cols_ps"), 1)

    def params_act(act):
        act.wait_ge(*S("cols_ps", 1))
        for g in range(4):
            n = GROUP_ROWS[g]
            last = act.copy(cols[:, g, 0:n], ps[3][:, g * P:g * P + n])
            last.then_inc(S("cols_ready"), 1)

    def turn_pe(pe, n, src):
        for b in range(4):
            tt, kh = b // 2, b % 2
            if n:
                pe.wait_ge(*S("rows_ready", 2 * (n - 1) + tt + 1))
            else:
                pe.wait_ge(*S("x_in", 16))
            for k in range(4):
                last = pe.transpose(ps[4 + b][:, k * P:k * P + P],
                                    src[:, tt, (4 * kh + k) * P:(4 * kh + k + 1) * P], ident)
            last.then_inc(S("turned"), 1)

    def feat(buf, b):
        tt, kh = b // 2, b % 2
        return buf[:, 4 * kh:4 * kh + 4, tt * P:tt * P + P]

    def turn_act(act, n, free_at):
        for b in range(4):
            if n:
                act.wait_ge(*S("shifted", 4 * (n - 1) + b + 1))
                src = tadd[:, b % 2, :].rearrange("p (a b) -> p a b", a=4)
            else:
                act.wait_ge(*S("turned", b + 1))
                src = bank(4 + b, 4)
            wait_from(act, *S("used", free_at))
            act.copy(feat(ah, b), src).then_inc(S("act_hi"), 1)

    def turn_dve(dve, n, scale=None):
        def lo(b):
            dve.wait_ge(*S("act_hi", 4 * n + b + 1))
            src = tadd[:, b % 2, :].rearrange("p (a b) -> p a b", a=4) if n else bank(4 + b, 4)
            dve.tensor_tensor(feat(al, b), src, feat(ah, b).bitcast(F32), ALU.subtract)\
               .then_inc(S("act_lo"), 1)
        for b in range(4):
            if n:
                if b >= 2:
                    lo(b - 2)
                dve.wait_ge(*S("turned", 4 * n + b + 1))
                dve.wait_ge(*S("act_lo", 4 * n + b - 1 if b >= 2 else 4 * n))
                g = scale(4 * (b % 2)).unsqueeze(2).to_broadcast([P, 4, P])
                dve.tensor_tensor(tadd[:, b % 2, :].rearrange("p (a b) -> p a b", a=4),
                                  bank(4 + b, 4), g, ALU.mult).then_inc(S("scaled"), 1)
            else:
                lo(b)
        if n:
            lo(2)
            lo(3)

    def turn_pool(pool, n, shift):
        for b in range(4):
            pool.wait_ge(*S("scaled", 4 * (n - 1) + b + 1))
            v = tadd[:, b % 2, :].rearrange("p (a b) -> p a b", a=4)
            pool.tensor_tensor(v, v, shift(4 * (b % 2)).unsqueeze(2).to_broadcast([P, 4, P]),
                               ALU.add).then_inc(S("shifted"), 1)

    bn = sm(48).rearrange("p (t h s) -> p t h s", t=2, h=4)
    mv = sm(4).rearrange("p (t s) -> p t s", t=2)
    rstd, nmr = sm(2), sm(2)

    def ln_sums_of_banks(dve, n, q):
        dve.wait_ge(*S("used", q.first + q.n))
        dve.wait_ge(*S("ln_done", 2 * n))
        for tt in range(TT):
            for h in range(2):
                c = slice(512 * h, 512 * h + 512)
                dve.scalar_tensor_tensor(x0[:, tt, c], x0[:, tt, c], ALPHA, ps[4 + 2 * tt + h][:, :],
                                         ALU.mult, ALU.add).then_inc(S("ln_sum"), 1)
                dve.wait_ge(*S("ln_sum", 4 * (n // 2) + 2 * tt + h + 1))
                dve.bn_stats(bn[:, tt, h, :], x0[:, tt, c]).then_inc(S("ln_stats"), 1)
            dve.wait_ge(*S("ln_stats", 4 * (n // 2) + 2 * tt + 2))
            dve.bn_aggr(mv[:, tt, :], bn[:, tt, 0:2, :].rearrange("p h s -> p (h s)"))\
               .then_inc(S("ln_aggr"), 1)

    def ln_sums_of_chunks(dve, n, q):
        for j in range(q.n):
            c = q.first + j
            slot, cc = c % RING, slice(CC * j, CC * j + CC)
            dve.wait_ge(*S("used", c + 1))
            wait_from(dve, *S("ln_done", 2 * n))
            dve.scalar_tensor_tensor(x0[:, :, cc], x0[:, :, cc], ALPHA, bank(slot, 2),
                                     ALU.mult, ALU.add).then_inc(S("taken"), 1)
            dve.wait_ge(*S("taken", q.before["taken"] + j + 1))
            for tt in range(TT):
                dve.bn_stats(bn[:, tt, j, :], x0[:, tt, cc]).then_inc(S("lnc_stats"), 1)
            cut_ahead(dve, q, j, slot, c // RING)
        dve.wait_ge(*S("lnc_stats", 8 * (n // 2 + 1)))
        for tt in range(TT):
            dve.bn_aggr(mv[:, tt, :], bn[:, tt, :, :].rearrange("p h s -> p (h s)"))\
               .then_inc(S("ln_aggr"), 1)

    def ln_rows(dve, n, rows_sem="rows_ready"):
        for tt in range(TT):
            dve.wait_ge(*S("ln_rstd", 2 * n + tt + 1))
            dve.tensor_scalar(nmr[:, tt:tt + 1], mv[:, tt, 0:1], rstd[:, tt:tt + 1], -1.0,
                              ALU.mult, ALU.mult).then_inc(S("ln_nmr"), 1)
            dve.wait_ge(*S("ln_nmr", 2 * n + tt + 1))
            dve.tensor_scalar(xn[:, tt, :], x0[:, tt, :], rstd[:, tt:tt + 1], nmr[:, tt:tt + 1],
                              ALU.mult, ALU.add).then_inc(S(rows_sem), 1)

    def ln_pool(pool, n):
        for tt in range(TT):
            pool.wait_ge(*S("ln_aggr", 2 * n + tt + 1))
            pool.wait_ge(*S("powers", 1))
            pool.tensor_scalar(rstd[:, tt:tt + 1], mv[:, tt, 1:2], LN_EPS, None, ALU.add)\
                .then_inc(S("ln_var"), 1)
            pool.wait_ge(*S("ln_var", 2 * n + tt + 1))
            pool.tensor_tensor(rstd[:, tt:tt + 1], rstd[:, tt:tt + 1], half_neg[:, 0:1], ALU.pow)\
                .then_inc(S("ln_rstd"), 1)

    def ln_affine_pool(pool, n, sem, count):
        for tt in range(TT):
            pool.wait_ge(*S(sem, count + tt + 1))
            pool.wait_ge(*S("gb_in", 32 * n + 32))
            pool.tensor_tensor(x0[:, tt, :], xn[:, tt, :], gb[:, 0, :], ALU.mult)\
                .then_inc(S("ln_scaled"), 1)
            pool.wait_ge(*S("ln_scaled", 2 * n + tt + 1))
            pool.tensor_tensor(x0[:, tt, :], x0[:, tt, :], gb[:, 1, :], ALU.add)\
                .then_inc(S("ln_done"), 1)

    def ln_rows_load(act, n, g, b):
        if n:
            act.wait_ge(*S("ln_done", 2 * n))
        act.dma_start(gb[:, 0, :], g.broadcast_to([P, D])).then_inc(S("gb_in"), 16)
        act.dma_start(gb[:, 1, :], b.broadcast_to([P, D])).then_inc(S("gb_in"), 16)

    fh = at("fh", 0, [P, KF, T], F32R)
    fl = at("fl", 22, [P, KF, T], F32R)
    f_sig = at("f_sig", 44, [P, RING, T])
    f_act = at("f_act", 74, [P, RING, T])

    def ffn_pe(pe, n, gate=None):
        stream_pe(pe, f"up{n}", ah, al)
        if gate is not None:
            gate_rows_pe(pe, gate)
        pe.wait_ge(*S("hid_lo", KF * (n + 1)))
        stream_pe(pe, f"down{n}", fh, fl)

    def ffn_act(act, n, gate=None):
        q = segs[f"up{n}"]

        def hi(j, slot):
            act.wait_ge(*S("hid", j + (KF * n + 1)))
            act.copy(fh[:, bass.ds(j, 1), :].rearrange("p a t -> p (a t)"), f_act[:, slot, :])\
               .then_inc(S("hid_hi"), 1)

        def body(j, slot, turn):
            act.wait_ge(*S("used", turn * RING + slot + 1))
            act.activation(f_sig[:, slot, :], ps[slot][:, 0:T], ACT.Silu).then_inc(S("silu"), 1)
            if not (isinstance(j, int) and j == 0):
                hi(j - 1, (slot - 1) % RING)
            cut_ahead(act, q, j, slot, turn)
        walk(act, q, body)
        hi(KF - 1, (q.first + KF - 1) % RING)
        if gate is not None:
            gate_rows_act(act, gate)
        q = segs[f"down{n}"]
        walk(act, q, lambda j, slot, turn: cut_ahead(act, q, j, slot, turn))

    def ffn_dve(dve, n):
        q = segs[f"up{n}"]

        def lo(j, slot):
            dve.wait_ge(*S("hid_hi", j + (KF * n + 1)))
            row = fh[:, bass.ds(j, 1), :].rearrange("p a t -> p (a t)")
            dve.tensor_tensor(fl[:, bass.ds(j, 1), :].rearrange("p a t -> p (a t)"), f_act[:, slot, :],
                              row.bitcast(F32), ALU.subtract).then_inc(S("hid_lo"), 1)

        def body(j, slot, turn):
            dve.wait_ge(*S("silu", j + (KF * n + 1)))
            wait_from(dve, *S("hid_lo", j + (KF * n - RING + 1)))
            dve.tensor_tensor(f_act[:, slot, :], ps[slot][:, T:2 * T], f_sig[:, slot, :], ALU.mult)\
               .then_inc(S("hid"), 1)
            if not (isinstance(j, int) and j == 0):
                lo(j - 1, (slot - 1) % RING)
            cut_ahead(dve, q, j, slot, turn)
        walk(dve, q, body)
        lo(KF - 1, (q.first + KF - 1) % RING)
        q = segs[f"down{n}"]
        walk(dve, q, lambda j, slot, turn: cut_ahead(dve, q, j, slot, turn))

    HG = 4
    qkv = at("qkv", 0, [P, 24, T])
    gz = at("gz", 24, [P, 8, T])
    conv_y = at("conv_y", 61, [P, RING, 2 * T])
    g_sq = at("g_sq", 44, [P, 16, T])
    state = at("state", 32, [P, 8, P])
    ktok = at("ktok", 36, [P, 8, P])
    vbeta = at("vbeta", 40, [P, 8, P])
    inv = at("inv", 44, [P, 8, P])
    invt = at("invt", 48, [P, 8, P])
    lowt = at("lowt", 52, [P, 8, P])
    attt = at("attt", 56, [P, 8, P])
    kbg = at("kbg", 60, [P, 8, P])
    dect = at("dect", 64, [P, 8, P])
    clev = at("clev", 68, [P, 2, HG, P])
    wlev = at("wlev", 72, [P, 2, HG, P])
    diag = nc.alloc_sbuf_tensor_at("diag", [P, 2, HG, P], F32, offset=base + 74 * 1024)
    x1f = x1[:, :, :].rearrange("p t d -> p (t d)")
    erow = x1f[:, 0:1024].rearrange("p (g a b) -> p g a b", g=2, a=HG)
    vnew = x1f[:, 1024:2048].rearrange("p (a b) -> p a b", a=8)
    g_o, g_u, g_wt = kbg, inv, lowt
    g_osq = at("g_osq", 68, [P, 8, P])

    ba = sm(32).rearrange("p (t c) -> p t c", t=2)
    g_norm = sm(32).rearrange("p (t c) -> p t c", t=2)
    beta = sm(16).rearrange("p (t c) -> p t c", t=2)
    g_exp, g_ln, g_max, g_g = (sm(16).rearrange("p (t c) -> p t c", t=2) for _ in range(4))
    g_cum = sm(32).rearrange("p (t c) -> p t c", t=2)
    g_egc, g_ekt = (sm(16).rearrange("p (t c) -> p t c", t=2) for _ in range(2))
    g_ea = sm(8)
    cdk = sm(32).rearrange("p (t h c) -> p t h c", t=2, h=8)
    g_rn = sm(8)

    def heads(g):
        return slice(HG * g, HG * g + HG)

    def over(mask):
        return mask.unsqueeze(1).to_broadcast([P, HG, P])

    def per_head(c):
        return c.unsqueeze(2).to_broadcast([P, HG, P])

    def small_weight_load(act, n, w, off):
        act.dma_start(g_raw[:, :, :], w.rearrange("(k p) n -> p k n", p=P)[:, :, off:off + 16])\
           .then_inc(S("gates_in"), 16)

    def small_weight_cut(dve, n):
        dve.wait_ge(*S("gates_in", 16 * (n + 1)))
        dve.tensor_copy(swh[:, :, :], g_raw[:, :, :]).then_inc(S("gates_cut"), 1)
        dve.wait_ge(*S("gates_cut", 2 * n + 1))
        dve.tensor_tensor(swl[:, :, :], g_raw[:, :, :], swh[:, :, :].bitcast(F32), ALU.subtract)\
           .then_inc(S("gates_cut"), 1)

    def gates_pe(pe, n, out_bank, free_sem=None, free=0):
        pe.wait_ge(*S("gates_cut", min(2 * n + 2, 4)))
        for tt in range(TT):
            pairs = []
            c = slice(tt * P, tt * P + P)
            for k in range(KD):
                pairs += [(ah[:, k, c], swh[:, k, :]), (ah[:, k, c], swl[:, k, :]),
                          (al[:, k, c], swh[:, k, :])]
            last = products(pe, ps[out_bank][:, 16 * tt:16 * tt + 16], pairs)
        last.then_inc(S("gates_ps"), 1)

    def gdn_in_pe(pe):
        pe.wait_ge(*S("act_lo", 4))
        gates_pe(pe, 0, 7)
        stream_pe(pe, "g_qkv", ah, al)
        stream_pe(pe, "g_z", ah, al)

    def gdn_in_act(act):
        q = segs["g_qkv"]

        def silu(j, slot):
            act.wait_ge(*S("taps", j * 5 + 5))
            act.wait_ge(*S("taken", j + 1))
            act.activation(qkv[:, bass.ds(j * 2, 2), :].rearrange("p a t -> p (a t)"),
                           conv_y[:, slot, :], ACT.Silu).then_inc(S("conv"), 1)

        def body(j, slot, turn):
            act.wait_ge(*S("used", turn * RING + slot + 1))
            wait_from(act, *S("conv", j - RING + 1))
            for f in range(2):
                act.activation(conv_y[:, slot, T * f:T * f + T], ps[slot][:, T * f:T * f + T], ACT.Copy,
                               scale=col("a_conv", j * 2 + (3 * 24 + f))).then_inc(S("tap3"), 1)
            if not (isinstance(j, int) and j == 0):
                silu(j - 1, (slot - 1) % RING)
            cut_ahead(act, q, j, slot, turn)
        walk(act, q, body)
        silu(q.n - 1, (q.first + q.n - 1) % RING)
        q = segs["g_z"]

        def body_z(j, slot, turn):
            act.wait_ge(*S("used", turn * RING + slot + 1))
            act.activation(gz[:, 2 * j:2 * j + 2, :].rearrange("p a t -> p (a t)"), ps[slot][:, :],
                           ACT.Silu).then_inc(S("taken"), 1)
            cut_ahead(act, q, j, slot, turn)
        walk(act, q, body_z)

    def gdn_in_dve(dve):
        q = segs["g_qkv"]
        small_weight_cut(dve, 0)

        def body(j, slot, turn):
            for s in (1, 2, 3):
                for f in range(2):
                    y = conv_y[:, slot, T * f + s:T * f + T]
                    if s == 1:
                        dve.wait_ge(*S("tap3", j * 2 + 2))
                    else:
                        dve.wait_ge(*S("taps", j * 5 + (2 * (s - 2) + f + 1)))
                    done = "taken" if (s, f) == (3, 1) else "taps"
                    dve.scalar_tensor_tensor(y, ps[slot][:, T * f:T * f + T - s],
                                             col("a_conv", j * 2 + ((3 - s) * 24 + f)), y,
                                             ALU.mult, ALU.add).then_inc(S(done), 1)
            cut_ahead(dve, q, j, slot, turn)
        walk(dve, q, body)
        q = segs["g_z"]
        walk(dve, q, lambda j, slot, turn: cut_ahead(dve, q, j, slot, turn))

    def gdn_in_pool(pool):
        with pool.Fori(0, 8) as j:
            pool.wait_ge(*S("conv", j + 1))
            v = qkv[:, bass.ds(j * 2, 2), :].rearrange("p a t -> p (a t)")
            pool.tensor_tensor(g_sq[:, bass.ds(j * 2, 2), :].rearrange("p a t -> p (a t)"), v, v,
                               ALU.mult).then_inc(S("squares"), 1)

    def gdn_prep_pe(pe):
        pe.wait_ge(*S("squares", 8))
        pe.wait_ge(*S("ba", 1))
        for tt in range(TT):
            for f in range(16):
                last = pe.matmul(ps[7][:, 64 + 16 * tt + f:64 + 16 * tt + f + 1],
                                 g_sq[:, f, tt * P:tt * P + P], ones[:, 0:1], start=True, stop=True)
        last.then_inc(S("norms_ps"), 1)
        pe.wait_ge(*S("g", 1))
        pe.wait_ge(*S("norms", 1))
        for tt in range(TT):
            pe.matmul(ps[7][:, 128 + 16 * tt:136 + 16 * tt], tab("u64"), g_g[:, tt, :],
                      start=True, stop=True)
            last = pe.matmul(ps[7][:, 136 + 16 * tt:144 + 16 * tt], tab("blk64"), g_g[:, tt, :],
                             start=True, stop=True)
        last.then_inc(S("cum_ps"), 1)
        for n in range(8):
            pe.wait_ge(*S("diag", n + 1))
            wait_from(pe, *S("normed", n - 1))
            if n < 2:
                pe.wait_ge(*S("taken", segs["g_z"].before["taken"] + 4))
            pe.matmul(ps[n % 2][:, :], ones, diag[:, n % 2, :, :].rearrange("p a b -> p (a b)"),
                      start=True, stop=True).then_inc(S("norm_rows"), 1)

    def gdn_prep_act(act):
        act.wait_ge(*S("params_in", 16 * N_PARAM_DMA))
        act.activation(g_ea, a_log, ACT.Exp).then_inc(S("exp_a"), 1)
        act.wait_ge(*S("ba", 2))
        act.activation(beta, ba[:, :, 0:8], ACT.Exp, scale=-1.0).then_inc(S("exp_b"), 1)
        act.activation(g_exp, g_exp, ACT.Exp, scale=-1.0).then_inc(S("exp_s"), 1)
        act.wait_ge(*S("exp_s", 1))
        act.activation(g_ln, g_exp, ACT.Ln, bias=1.0).then_inc(S("ln_s"), 1)
        act.wait_ge(*S("cum", 2))
        act.activation(g_egc, g_cum[:, :, 0:8], ACT.Exp).then_inc(S("egc"), 1)
        act.activation(g_ekt, g_ekt, ACT.Exp).then_inc(S("ekt"), 1)

    def gdn_prep_dve(dve):
        dve.wait_ge(*S("gates_ps", 1))
        dve.tensor_copy(ba, ps[7][:, 0:32].rearrange("p (t c) -> p t c", t=2)).then_inc(S("ba"), 1)
        dve.wait_ge(*S("ba", 1))
        dve.wait_ge(*S("params_in", 16 * N_PARAM_DMA))
        dve.tensor_tensor(ba[:, :, 8:16], ba[:, :, 8:16],
                          dt_bias.unsqueeze(1).to_broadcast([P, 2, 8]), ALU.add).then_inc(S("soft"), 1)
        dve.wait_ge(*S("soft", 1))
        dve.tensor_scalar(g_max, ba[:, :, 8:16], 0.0, None, ALU.max).then_inc(S("soft"), 1)
        dve.tensor_scalar(g_exp, ba[:, :, 8:16], -1.0, None, ALU.mult).then_inc(S("soft"), 1)
        dve.wait_ge(*S("soft", 3))
        dve.tensor_tensor(g_exp, g_exp, ba[:, :, 8:16], ALU.max).then_inc(S("ba"), 1)
        dve.wait_ge(*S("exp_b", 1))
        dve.tensor_scalar(beta, beta, 1.0, None, ALU.add).then_inc(S("soft"), 1)
        dve.wait_ge(*S("soft", 4))
        dve.reciprocal(beta, beta).then_inc(S("beta"), 1)
        dve.wait_ge(*S("ln_s", 1))
        dve.tensor_tensor(g_ln, g_ln, g_max, ALU.add).then_inc(S("soft"), 1)
        dve.wait_ge(*S("soft", 5))
        dve.wait_ge(*S("exp_a", 1))
        dve.scalar_tensor_tensor(g_g, g_ln, -1.0, g_ea.unsqueeze(1).to_broadcast([P, 2, 8]),
                                 ALU.mult, ALU.mult).then_inc(S("g"), 1)
        dve.wait_ge(*S("norms_ps", 1))
        dve.tensor_scalar(g_norm, ps[7][:, 64:96].rearrange("p (t c) -> p t c", t=2), EPS, None,
                          ALU.add).then_inc(S("norms"), 1)
        dve.wait_ge(*S("cum_ps", 1))
        dve.tensor_copy(g_cum, ps[7][:, 128:160].rearrange("p (t c) -> p t c", t=2))\
           .then_inc(S("cum"), 1)
        dve.wait_ge(*S("cum", 1))
        dve.tensor_tensor(g_ekt, g_cum[:, :, 8:16], g_cum[:, :, 0:8], ALU.subtract)\
           .then_inc(S("cum"), 1)
        dve.wait_ge(*S("egc", 1))
        dve.wait_ge(*S("beta", 1))
        dve.tensor_tensor(g_egc, g_egc, beta, ALU.mult).then_inc(S("bexp"), 1)
        for n in range(8):
            tt, kind, g = n // 4, n // 2 % 2, n % 2
            dve.wait_ge(*S("norm_rows", n + 1))
            v = qkv[:, 8 * kind + HG * g:8 * kind + HG * g + HG, tt * P:tt * P + P]
            dve.tensor_tensor(v, v, bank(n % 2, HG), ALU.mult).then_inc(S("normed"), 1)

    def gdn_prep_pool(pool):
        pool.wait_ge(*S("norms", 1))
        pool.tensor_tensor(g_norm, g_norm, half_neg.rearrange("p (t c) -> p t c", t=2), ALU.pow)\
            .then_inc(S("norm"), 1)
        pool.wait_ge(*S("norm", 1))
        pool.tensor_scalar(g_norm[:, :, 0:8], g_norm[:, :, 0:8], float(P) ** -0.5, None, ALU.mult)\
            .then_inc(S("norm"), 1)
        pool.wait_ge(*S("norm", 2))
        for n in range(8):
            tt, kind, g = n // 4, n // 2 % 2, n % 2
            wait_from(pool, *S("norm_rows", n - 1))
            c = g_norm[:, tt, 8 * kind + HG * g:8 * kind + HG * g + HG]
            pool.tensor_tensor(diag[:, n % 2, :, :], over(ident), per_head(c), ALU.mult)\
                .then_inc(S("diag"), 1)
        pool.memset(state[:, :, :], 0.0).then_inc(S("state"), 1)

    def flat(ap):
        return ap.rearrange("p a b -> p (a b)")

    def gdn_tokens_pe(pe, tt):
        tile = slice(tt * P, tt * P + P)
        for g in range(2):
            n = 2 * tt + g
            pe.wait_ge(*S("diag_g", n + 1))
            pe.wait_ge(*S("normed", 8))
            wait_from(pe, *S("erow", n))
            wait_from(pe, *S("dt_diff", n))
            wait_from(pe, *S("lowt", n))
            if tt == 1 and g == 0:
                pe.wait_ge(*S("g_hi", 2))
                pe.wait_ge(*S("g_lo", 2))
            pe.matmul(ps[0][:, :], ones, flat(diag[:, 0, :, :]), start=True, stop=True)\
                .then_inc(S("row_ps"), 1)
            pe.wait_ge(*S("diag_b", n + 1))
            pe.matmul(ps[1][:, :], ones, flat(diag[:, 1, :, :]), start=True, stop=True)\
                .then_inc(S("rowb_ps"), 1)
            wait_from(pe, *S("att", n))
            wait_from(pe, *S("low0", n))
            wait_from(pe, *S("o", 2 * 2 * tt))
            wait_from(pe, *S("st", 2 * 2 * tt))
            for h in range(HG):
                pe.matmul(bank(2, HG)[:, h, :], qkv[:, 8 + HG * g + h, tile],
                          qkv[:, HG * g + h, tile], start=True, stop=True)
                last = pe.matmul(bank(4, HG)[:, h, :], qkv[:, 8 + HG * g + h, tile],
                                 qkv[:, 8 + HG * g + h, tile], start=True, stop=True)
            last.then_inc(S("qk_ps"), 1)
            wait_from(pe, *S("ktok", n))
            wait_from(pe, *S("vbeta", n))
            for h in range(HG):
                pe.transpose(bank(5, HG)[:, h, :], qkv[:, 8 + HG * g + h, tile], ident)
                last = pe.transpose(bank(6, HG)[:, h, :], qkv[:, 16 + HG * g + h, tile], ident)
            last.then_inc(S("kv_ps"), 1)
        for g in range(2):
            pe.wait_ge(*S("inv0", 2 * tt + g + 1))
            if g == 0:
                pe.wait_ge(*S("lowt", 2 * tt + 2))
                pe.wait_ge(*S("erow", 2 * tt + 2))
            for h in range(HG):
                last = pe.transpose(bank(g, HG)[:, h, :], invt[:, HG * g + h, :], ident)
            last.then_inc(S("inv0_ps"), 1)
        for s in range(1, 6):
            for g in range(2):
                n = 10 * tt + 2 * (s - 1) + g
                pe.wait_ge(*S("clev", n + 1))
                pe.wait_ge(*S("invcopy", 2 * tt + g + 1))
                wait_from(pe, *S("invup", 8 * tt + 2 * (s - 1) + g - 1 if s > 1 else 0))
                wait_from(pe, *S("wlev", n - 1))
                for h in range(HG):
                    last = pe.matmul(bank(g, HG)[:, h, :], clev[:, g, h, :], inv[:, HG * g + h, :],
                                     start=True, stop=True)
                last.then_inc(S("w_ps"), 1)
            for g in range(2):
                n = 10 * tt + 2 * (s - 1) + g
                pe.wait_ge(*S("wlev", n + 1))
                wait_from(pe, *S("invtup", n - 1))
                if s == 1:
                    pe.wait_ge(*S("vbeta", 2 * tt + 2))
                    pe.wait_ge(*S("ktok", 2 * tt + 2))
                    pe.wait_ge(*S("att", 2 * tt + 2))
                    pe.wait_ge(*S("low0", 2 * tt + 2))
                y, z = (2, 4) if g == 0 else (5, 6)
                for h in range(HG):
                    if s < 5:
                        pe.matmul(bank(y, HG)[:, h, :], invt[:, HG * g + h, :], wlev[:, g, h, :],
                                  start=True, stop=True)
                    last = pe.matmul(bank(z, HG)[:, h, :], wlev[:, g, h, :], invt[:, HG * g + h, :],
                                     start=True, stop=True)
                last.then_inc(S("twt_ps"), 1)
        for g in range(2):
            pe.wait_ge(*S("invtup", 10 * tt + 9 + g))
            pe.wait_ge(*S("kbg", 2 * tt + g + 1))
            for h in range(HG):
                pe.matmul(bank(g, HG)[:, h, :], invt[:, HG * g + h, :], vbeta[:, HG * g + h, :],
                          start=True, stop=True)
                last = pe.matmul(bank(2 if g == 0 else 5, HG)[:, h, :], kbg[:, HG * g + h, :],
                                 invt[:, HG * g + h, :], start=True, stop=True)
            last.then_inc(S("uw_ps"), 1)
        for i in range(2):
            c = slice(64 * i, 64 * i + 64)
            for g in range(2):
                n = 4 * tt + 2 * i + g
                pe.wait_ge(*S("uw", 2 * (2 * tt + 2)))
                pe.wait_ge(*S("st", n - g if n - g > 0 else 0)) if n - g > 0 else \
                    pe.wait_ge(*S("state", 1))
                wait_from(pe, *S("vnew", 2 * (2 * tt + i)))
                for h in range(HG):
                    last = pe.matmul(bank(g, HG)[c, h, :], g_wt[:, HG * g + h, c],
                                     state[:, HG * g + h, :], start=True, stop=True)
                last.then_inc(S("v_ps"), 1)
            for g in range(2):
                n = 4 * tt + 2 * i + g
                pe.wait_ge(*S("vnew", n + 1))
                pe.wait_ge(*S("qdec", 2 * tt + g + 1))
                wait_from(pe, *S("o", 4 * tt + 2 * i))
                for h in range(HG):
                    o = bank(2 if g == 0 else 4, HG)[c, h, :]
                    pe.matmul(o, qkv[:, HG * g + h, tt * P + 64 * i:tt * P + 64 * i + 64],
                              state[:, HG * g + h, :], start=True, stop=False)
                    last = pe.matmul(o, attt[c, HG * g + h, c], vnew[c, HG * g + h, :],
                                     start=False, stop=True)
                last.then_inc(S("o_ps"), 1)
                pe.wait_ge(*S("kd", 2 * tt + g + 1))
                wait_from(pe, *S("st", 4 * tt + 2 * i))
                for h in range(HG):
                    last = pe.matmul(bank(5 + g, HG)[:, h, :], ktok[c, HG * g + h, :],
                                     vnew[c, HG * g + h, :], start=True, stop=True)
                last.then_inc(S("s_ps"), 1)
        for g in range(2):
            pe.wait_ge(*S("onorm", tt + 1))
            for h in range(HG):
                last = pe.transpose(bank(g, HG)[:, h, :], g_o[:, HG * g + h, :], ident)
            last.then_inc(S("ot_ps"), 1)

    def gdn_tokens_act(act, tt):
        for g in range(2):
            n = 2 * tt + g
            act.wait_ge(*S("dt_diff", n + 1))
            wait_from(act, *S("qdec", n - 1))
            wait_from(act, *S("cdk", n - 1))
            act.activation(erow[:, g, :, :], bank(0, HG), ACT.Exp).then_inc(S("erow"), 1)
            act.wait_ge(*S("dt_m1", n + 1))
            act.activation(dect[:, heads(g), :], dect[:, heads(g), :], ACT.Exp)\
               .then_inc(S("dt_exp"), 1)
            act.wait_ge(*S("kv_ps", n + 1))
            act.copy(ktok[:, heads(g), :], bank(5, HG)).then_inc(S("ktok"), 1)
        for g in range(2):
            act.wait_ge(*S("inv0_ps", 2 * tt + g + 1))
            act.copy(inv[:, heads(g), :], bank(g, HG)).then_inc(S("invcopy"), 1)
        for s in range(1, 6):
            for g in range(2):
                n = 10 * tt + 2 * (s - 1) + g
                act.wait_ge(*S("w_ps", n + 1))
                wait_from(act, *S("twt_ps", n - 1))
                act.copy(wlev[:, g, :, :], bank(g, HG)).then_inc(S("wlev"), 1)
        for g in range(2):
            act.wait_ge(*S("uw_ps", 2 * tt + g + 1))
            act.copy(g_u[:, heads(g), :], bank(g, HG)).then_inc(S("uw"), 1)
            act.copy(g_wt[:, heads(g), :], bank(2 if g == 0 else 5, HG)).then_inc(S("uw"), 1)
        for i in range(2):
            c = slice(64 * i, 64 * i + 64)
            for g in range(2):
                act.wait_ge(*S("o_ps", 4 * tt + 2 * i + g + 1))
                act.copy(g_o[c, heads(g), :], bank(2 if g == 0 else 4, HG)[c, :, :])\
                   .then_inc(S("o"), 1)
        for g in range(2):
            act.wait_ge(*S("gated", 2 * tt + g + 1))
            act.copy(ah[:, heads(g), tt * P:tt * P + P], g_gated(g)).then_inc(S("g_hi"), 1)

    def g_gated(g):
        return diag[:, g, :, :]

    def gdn_tokens_dve(dve, tt):
        tile = slice(tt * P, tt * P + P)
        for g in range(2):
            n = 2 * tt + g
            h = heads(g)
            dve.wait_ge(*S("row_ps", n + 1))
            dve.tensor_tensor(dect[:, h, :], bank(0, HG), per_head(g_cum[:, tt, HG * g:HG * g + HG]),
                              ALU.subtract).then_inc(S("dt_diff"), 1)
            dve.wait_ge(*S("kv_ps", n + 1))
            dve.tensor_tensor(vbeta[:, h, :], bank(6, HG), per_head(beta[:, tt, HG * g:HG * g + HG]),
                              ALU.mult).then_inc(S("vbeta"), 1)
            dve.wait_ge(*S("erow", n + 1))
            dve.tensor_copy(cdk[:, tt, h, :], erow[:, g, :, 63::64]).then_inc(S("cdk"), 1)
            dve.wait_ge(*S("qk_ps", n + 1))
            v = qkv[:, h, tile]
            dve.tensor_tensor(v, v, erow[:, g, :, :], ALU.mult).then_inc(S("qdec"), 1)
            dve.wait_ge(*S("dt", n + 1))
            dve.tensor_tensor(lowt[:, h, :], bank(4, HG), dect[:, h, :], ALU.mult)\
               .then_inc(S("low0"), 1)
            dve.tensor_tensor(attt[:, h, :], bank(2, HG), dect[:, h, :], ALU.mult)\
               .then_inc(S("att"), 1)
            dve.wait_ge(*S("low1", n + 1))
            dve.wait_ge(*S("rowb_ps", n + 1))
            dve.tensor_tensor(lowt[:, h, :], lowt[:, h, :], bank(1, HG), ALU.mult)\
               .then_inc(S("lowt"), 1)
        for g in range(2):
            dve.wait_ge(*S("clev0", 2 * tt + g + 1))
            dve.tensor_tensor(invt[:, heads(g), :], over(ident), clev[:, g, :, :], ALU.subtract)\
               .then_inc(S("inv0"), 1)
        for s in range(1, 6):
            for g in range(2):
                n = 10 * tt + 2 * (s - 1) + g
                y, z = (2, 4) if g == 0 else (5, 6)
                h = heads(g)
                dve.wait_ge(*S("twt_ps", n + 1))
                if s < 5:
                    dve.tensor_tensor(inv[:, h, :], inv[:, h, :], bank(y, HG), ALU.subtract)\
                       .then_inc(S("invup"), 1)
                dve.tensor_tensor(invt[:, h, :], invt[:, h, :], bank(z, HG), ALU.subtract)\
                   .then_inc(S("invtup"), 1)
        for i in range(2):
            c = slice(64 * i, 64 * i + 64)
            for g in range(2):
                n = 4 * tt + 2 * i + g
                dve.wait_ge(*S("v_ps", n + 1))
                dve.wait_ge(*S("uw", 4 * tt + 4))
                dve.tensor_tensor(vnew[c, heads(g), :], g_u[c, heads(g), :], bank(g, HG)[c, :, :],
                                  ALU.subtract).then_inc(S("vnew"), 1)
            for g in range(2):
                n = 4 * tt + 2 * i + g
                dve.wait_ge(*S("st_dec", n + 1))
                dve.wait_ge(*S("s_ps", n + 1))
                dve.tensor_tensor(state[:, heads(g), :], state[:, heads(g), :], bank(5 + g, HG),
                                  ALU.add).then_inc(S("st"), 1)
        dve.wait_ge(*S("osq", tt + 1))
        dve.tensor_reduce(g_rn, g_osq[:, :, :], AX, ALU.add).then_inc(S("osum"), 1)
        dve.wait_ge(*S("orn", tt + 1))
        dve.tensor_tensor(g_o[:, :, :], g_o[:, :, :], g_rn.unsqueeze(2).to_broadcast([P, 8, P]),
                          ALU.mult).then_inc(S("onorm"), 1)
        for g in range(2):
            dve.wait_ge(*S("ot_ps", 2 * tt + g + 1))
            dve.scalar_tensor_tensor(g_gated(g), bank(g, HG), col("a_norm"), gz[:, heads(g), tile],
                                     ALU.mult, ALU.mult).then_inc(S("gated"), 1)
        for g in range(2):
            dve.wait_ge(*S("g_hi", 2 * tt + g + 1))
            dve.tensor_tensor(al[:, heads(g), tile], g_gated(g), ah[:, heads(g), tile].bitcast(F32),
                              ALU.subtract).then_inc(S("g_lo"), 1)

    def gdn_tokens_pool(pool, tt):
        for g in range(2):
            n = 2 * tt + g
            gs = slice(HG * g, HG * g + HG)
            h = heads(g)
            if g == 1:
                pool.wait_ge(*S("rowb_ps", n))
            else:
                pool.wait_ge(*S("normed", 8))
                wait_from(pool, *S("g_lo", 2 * tt))
            pool.tensor_tensor(diag[:, 0, :, :], over(tab("u64")), per_head(g_g[:, tt, gs]), ALU.mult)\
                .then_inc(S("diag_g"), 1)
            pool.tensor_tensor(diag[:, 1, :, :], over(ident), per_head(beta[:, tt, gs]), ALU.mult)\
                .then_inc(S("diag_b"), 1)
            pool.wait_ge(*S("dt_diff", n + 1))
            pool.tensor_tensor(dect[:, h, :], dect[:, h, :], over(tab("u64")), ALU.mult)\
                .then_inc(S("dt_m1"), 1)
            pool.wait_ge(*S("ktok", n + 1))
            pool.wait_ge(*S("bexp", 1))
            pool.tensor_tensor(kbg[:, h, :], ktok[:, h, :], per_head(g_egc[:, tt, gs]), ALU.mult)\
                .then_inc(S("kbg"), 1)
            pool.wait_ge(*S("dt_exp", n + 1))
            pool.tensor_tensor(dect[:, h, :], dect[:, h, :], over(tab("u64")), ALU.mult)\
                .then_inc(S("dt"), 1)
            pool.wait_ge(*S("kbg", n + 1))
            pool.wait_ge(*S("ekt", 1))
            pool.tensor_tensor(ktok[:, h, :], ktok[:, h, :], per_head(g_ekt[:, tt, gs]), ALU.mult)\
                .then_inc(S("kd"), 1)
            pool.wait_ge(*S("low0", n + 1))
            pool.tensor_tensor(lowt[:, h, :], lowt[:, h, :], over(tab("us64")), ALU.mult)\
                .then_inc(S("low1"), 1)
        for s in range(6):
            for g in range(2):
                pool.wait_ge(*S("lowt", 2 * tt + g + 1))
                if s == 1:
                    pool.wait_ge(*S("inv0", 2 * tt + g + 1))
                if s > 1:
                    pool.wait_ge(*S("w_ps", 10 * tt + 2 * (s - 2) + g + 1))
                if s == 0:
                    wait_from(pool, *S("orn", tt))
                pool.tensor_tensor(clev[:, g, :, :], lowt[:, heads(g), :],
                                   over(tab("level", 6)[:, s, :]), ALU.mult)\
                    .then_inc(S("clev" if s else "clev0"), 1)
        for i in range(2):
            for g in range(2):
                n = 4 * tt + 2 * i + g
                pool.wait_ge(*S("o_ps", n + 1))
                pool.tensor_tensor(state[:, heads(g), :], state[:, heads(g), :],
                                   per_head(cdk[:, tt, heads(g), i]), ALU.mult)\
                    .then_inc(S("st_dec"), 1)
        pool.wait_ge(*S("o", 4 * tt + 4))
        pool.wait_ge(*S("clev", 10 * tt + 10))
        pool.wait_ge(*S("twt_ps", 10 * tt + 10))
        pool.tensor_tensor(g_osq[:, :, :], g_o[:, :, :], g_o[:, :, :], ALU.mult).then_inc(S("osq"), 1)
        pool.wait_ge(*S("osum", tt + 1))
        pool.tensor_scalar(g_rn, g_rn, 1.0 / P, EPS, ALU.mult, ALU.add).then_inc(S("omean"), 1)
        pool.wait_ge(*S("omean", tt + 1))
        pool.tensor_tensor(g_rn, g_rn, half_neg[:, 0:8], ALU.pow).then_inc(S("orn"), 1)

    a_qk = at("a_qk", 0, [P, TT, 2048])
    a_v = at("a_v", 16, [P, TT, D])
    a_t = at("a_t", 24, [P, 16, T])
    a_rope = at("a_rope", 40, [P, 4, 16, 16])
    a_s = at("a_s", 44, [P, 2, 384])
    a_pt = at("a_pt", 47, [P, 2, 384])
    a_o = at("a_o", 50, [P, 2, T])
    a_max = sm(4).rearrange("p (s t) -> p s t", s=2)
    a_sum = sm(4).rearrange("p (s t) -> p s t", s=2)
    A_SCALE = float(P) ** -0.5

    def att_in_pe(pe):
        pe.wait_ge(*S("act_lo", 12))
        stream_pe(pe, "m_qkv", ah, al)

    def att_in_act(act):
        q = segs["m_qkv"]
        base_t = q.before["taken"]

        def body(j, slot, turn):
            act.wait_ge(*S("used", turn * RING + slot + 1))
            if isinstance(j, int) and j >= 8:
                dst = a_v[:, :, CC * (j - 8):CC * (j - 8) + CC]
            else:
                dst = a_qk[:, :, bass.ds(j * CC, CC)]
            act.copy(dst, bank(slot, 2)).then_inc(S("taken"), 1)
            cut_ahead(act, q, j, slot, turn)
        for j in range(q.n):
            c = q.first + j
            body(j, c % RING, c // RING)

    def att_in_dve(dve):
        q = segs["m_qkv"]
        walk(dve, q, lambda j, slot, turn: cut_ahead(dve, q, j, slot, turn))
        rope = tab("rope").rearrange("p (t c d) -> p t c d", t=2, c=2)
        dve.wait_ge(*S("taken", q.before["taken"] + 8))
        for tt in range(TT):
            v = a_qk[:, tt, :].rearrange("p (h d) -> p h d", h=16)
            lo, hi = v[:, :, 0:16], v[:, :, 16:32]
            cos = rope[:, tt, 0, :].unsqueeze(1).to_broadcast([P, 16, 16])
            sin = rope[:, tt, 1, :].unsqueeze(1).to_broadcast([P, 16, 16])
            wait_from(dve, *S("roped", 2 * tt))
            for i, (a, b) in enumerate([(lo, cos), (hi, sin), (lo, sin), (hi, cos)]):
                dve.tensor_tensor(a_rope[:, i, :, :], a, b, ALU.mult).then_inc(S("rotated"), 1)
            dve.wait_ge(*S("rotated", 4 * tt + 4))
            dve.tensor_tensor(lo, a_rope[:, 0, :, :], a_rope[:, 1, :, :], ALU.subtract)\
               .then_inc(S("roped"), 1)
            dve.tensor_tensor(hi, a_rope[:, 2, :, :], a_rope[:, 3, :, :], ALU.add)\
               .then_inc(S("roped"), 1)

    ATT_BANKS = (4, 5, 6, 7)

    def att_pe(pe):
        for n in range(8):
            tt, g = n // 4, n % 4
            pe.wait_ge(*S("roped", 2 * tt + 2))
            wait_from(pe, *S("qkt", n - 3))
            for h in range(HG):
                f = HG * g + h
                last = pe.transpose(ps[ATT_BANKS[n % 4]][:, h * P:h * P + P],
                                    a_qk[:, tt, f * P:f * P + P], ident)
            last.then_inc(S("qkt_ps"), 1)
        pe.wait_ge(*S("taken", segs["m_qkv"].before["taken"] + 12))

        def scores(h):
            if h == 0:
                pe.wait_ge(*S("qkt", 8))
            wait_from(pe, *S("scored", h - 1))
            b = ps[4 + h % 2]
            pe.matmul(b[:, 0:P], a_t[:, h, 0:P], a_t[:, 8 + h, 0:P], start=True, stop=True)
            pe.matmul(b[:, P:384], a_t[:, h, P:T], a_t[:, 8 + h, :], start=True, stop=True)\
                .then_inc(S("scores"), 1)

        def values(h):
            pe.wait_ge(*S("probs", h + 1))
            wait_from(pe, *S("pt", h - 1))
            for i in range(3):
                last = pe.transpose(ps[6][:, i * P:i * P + P] if h % 2 == 0 else
                                    ps[7][:, i * P:i * P + P], a_s[:, h % 2, i * P:i * P + P], ident)
            last.then_inc(S("pt_ps"), 1)
            pe.wait_ge(*S("pt", h + 1))
            wait_from(pe, *S("o_hi", h - 1))
            wait_from(pe, *S("o_copy", h - 1))
            b = ps[h % 2]
            c = slice(h * P, h * P + P)
            pt = a_pt[:, h % 2, :]
            pe.matmul(b[:, 0:P], a_v[:, 0, c], pt[:, 0:P], start=True, stop=True)
            pe.matmul(b[:, P:T], a_v[:, 0, c], pt[:, P:2 * P], start=True, stop=False)
            pe.matmul(b[:, P:T], a_v[:, 1, c], pt[:, 2 * P:3 * P], start=False, stop=True)\
                .then_inc(S("att_o"), 1)
        scores(0)
        for h in range(8):
            if h < 7:
                scores(h + 1)
            values(h)

    def att_act(act):
        for n in range(8):
            tt, g = n // 4, n % 4
            act.wait_ge(*S("qkt_ps", n + 1))
            act.copy(a_t[:, HG * g:HG * g + HG, tt * P:tt * P + P], bank(ATT_BANKS[n % 4], HG))\
               .then_inc(S("qkt"), 1)

        def out_parts(h):
            act.wait_ge(*S("att_o", h + 1))
            wait_from(act, *S("o_lo", h - 1))
            act.copy(a_o[:, h % 2, :], ps[h % 2][:, 0:T]).then_inc(S("o_copy"), 1)
            act.wait_ge(*S("o_copy", h + 1))
            act.copy(ah[:, h, :], a_o[:, h % 2, :]).then_inc(S("o_hi"), 1)

        for h in range(8):
            act.wait_ge(*S("row_max", h + 1))
            for tt, c in ((0, slice(0, P)), (1, slice(P, 384))):
                act.activation(a_s[:, h % 2, c], a_s[:, h % 2, c], ACT.Exp,
                               bias=a_max[:, h % 2, tt:tt + 1], accum_out=a_sum[:, h % 2, tt:tt + 1])\
                   .then_inc(S("exps"), 1)
            act.wait_ge(*S("pt_ps", h + 1))
            wait_from(act, *S("att_o", h - 1))
            act.copy(a_pt[:, h % 2, :], ps[6 + h % 2][:, 0:384]).then_inc(S("pt"), 1)
            if h:
                out_parts(h - 1)
        out_parts(7)

    def att_dve(dve):
        for h in range(8):
            s = a_s[:, h % 2, :]
            dve.wait_ge(*S("scores", h + 1))
            wait_from(dve, *S("pt_ps", h - 1))
            dve.scalar_tensor_tensor(s, ps[4 + h % 2][:, 0:384], A_SCALE, tab("causal"),
                                     ALU.mult, ALU.add).then_inc(S("scored"), 1)
            dve.wait_ge(*S("scored", h + 1))
            for tt, c in ((0, slice(0, P)), (1, slice(P, 384))):
                dve.tensor_reduce(a_max[:, h % 2, tt:tt + 1], s[:, c], AX, ALU.max)\
                   .then_inc(S("maxes"), 1)
            dve.wait_ge(*S("maxes", 2 * h + 2))
            dve.tensor_scalar(a_max[:, h % 2, :], a_max[:, h % 2, :], -1.0, None, ALU.mult)\
               .then_inc(S("row_max"), 1)
            dve.wait_ge(*S("exps", 2 * h + 2))
            dve.reciprocal(a_sum[:, h % 2, :], a_sum[:, h % 2, :]).then_inc(S("inv_sum"), 1)
            dve.wait_ge(*S("inv_sum", h + 1))
            dve.tensor_scalar(s[:, 0:P], s[:, 0:P], a_sum[:, h % 2, 0:1], None, ALU.mult)\
               .then_inc(S("probs0"), 1)
            dve.wait_ge(*S("probs0", h + 1))
            dve.tensor_scalar(s[:, P:384], s[:, P:384], a_sum[:, h % 2, 1:2], None, ALU.mult)\
               .then_inc(S("probs"), 1)
            if h:
                lo_part(dve, h - 1)
        lo_part(dve, 7)

    def lo_part(dve, h):
        dve.wait_ge(*S("o_hi", h + 1))
        dve.tensor_tensor(al[:, h, :], a_o[:, h % 2, :], ah[:, h, :].bitcast(F32), ALU.subtract)\
           .then_inc(S("o_lo"), 1)

    ADA = 9 * D // CC
    ada_raw = at("ada_raw", 0, [P, 2, CHUNK])
    ada_row = at("ada_row", 16, [P, 2, CC])
    silu_c = at("silu_c", 18, [P, KD, 2])
    ada = adat[:, :].rearrange("p (f w) -> p f w", w=2)
    mod_g = sm(40).rearrange("p (i k) -> p i k", k=8)
    gate_c = sm(32).rearrange("p (i k) -> p i k", k=8)
    MODS = [(1, 1, 0, 0), (1, 4, 3, 2), (0, 1, 0, 0), (0, 4, 3, 2), (0, 7, 6, 4)]
    GATES = [(1, 2, 1, 0.5), (0, 2, 1, 0.5), (0, 5, 3, 1.0), (0, 8, 5, 0.5)]

    def ada_pool(pool):
        v = A["w_ada_2"][0].rearrange("(k p) n -> p k n", p=P)
        pool.wait_ge(*S("used", segs["down1"].first + segs["down1"].n))
        for slot in range(2):
            pool.dma_start(ada_raw[:, slot, :].rearrange("p (k n) -> p k n", k=KD),
                           v[:, :, slot * CC:slot * CC + CC]).then_inc(S(f"ada_in{slot}"), 16)
        with pool.Fori(1, ADA // 2) as i:
            for slot in range(2):
                pool.wait_ge(*S("ada_ps", i * 2 + (slot - 1)))
                pool.dma_start(ada_raw[:, slot, :].rearrange("p (k n) -> p k n", k=KD),
                               v[:, :, bass.ds(i * (2 * CC) + slot * CC, CC)])\
                    .then_inc(S(f"ada_in{slot}"), 16)
        pool.dma_start(x1[:, :, :], A["ctx_2"][0].rearrange("(t p) d -> p t d", p=P))\
            .then_inc(S("ctx_in"), 16)

    def ada_pe(pe):
        pe.wait_ge(*S("silu_c", 2))

        def chunk(c, slot, turn):
            pe.wait_ge(*S(f"ada_in{slot}", turn * 16 + 16))
            wait_from(pe, *S("ada_row", c - 1))
            w = ada_raw[:, slot, :].rearrange("p (k n) -> p k n", k=KD)
            for k in range(KD):
                last = pe.matmul(ps[slot][0:2, 0:CC], silu_c[:, k, :], w[:, k, :],
                                 start=(k == 0), stop=(k == KD - 1))
            last.then_inc(S("ada_ps"), 1)

        def to_columns(c, slot):
            pe.wait_ge(*S("ada_row", c + 1))
            for f in range(2):
                last = pe.matmul(ps[2][:, bass.ds(c * 4 + 2 * f, 2)],
                                 ada_row[0:2, slot, f * P:f * P + P], ident[0:2, 0:2],
                                 start=True, stop=True)
            last.then_inc(S("ada_cols"), 1)
        chunk(0, 0, 0)
        chunk(1, 1, 0)
        to_columns(0, 0)
        with pe.Fori(1, ADA // 2) as i:
            chunk(i * 2, 0, i)
            to_columns(i * 2 - 1, 1)
            chunk(i * 2 + 1, 1, i)
            to_columns(i * 2, 0)
        to_columns(ADA - 1, 1)

    def ada_act(act):
        act.wait_ge(*S("used", segs["down1"].first + segs["down1"].n))
        act.activation(silu_c[:, :, 0], col("c", 0, 8), ACT.Silu).then_inc(S("silu_c"), 1)
        act.activation(silu_c[:, :, 1], col("c_ctx", 0, 8), ACT.Silu).then_inc(S("silu_c"), 1)

        def row(c, slot):
            act.wait_ge(*S("ada_ps", c + 1))
            wait_from(act, *S("ada_cols", c - 1))
            act.copy(ada_row[0:2, slot, :], ps[slot][0:2, 0:CC]).then_inc(S("ada_row"), 1)
        row(0, 0)
        row(1, 1)
        with act.Fori(1, ADA // 2) as i:
            row(i * 2, 0)
            row(i * 2 + 1, 1)

    def ada_dve(dve):
        dve.wait_ge(*S("ada_cols", ADA))
        dve.tensor_tensor(ada, ps[2][:, 0:144].rearrange("p (f w) -> p f w", w=2),
                          col("b_ada", 0, 72).unsqueeze(2).to_broadcast([P, 72, 2]), ALU.add)\
           .then_inc(S("ada"), 1)
        dve.wait_ge(*S("ada", 1))
        for i, (w, scale, _, g) in enumerate(MODS):
            dve.scalar_tensor_tensor(mod_g[:, i, :], ada[:, 8 * scale:8 * scale + 8, w], 1.0,
                                     col("norm_g", 8 * g, 8), ALU.add, ALU.mult).then_inc(S("mods"), 1)
        for i, (w, gate, g, factor) in enumerate(GATES):
            dve.scalar_tensor_tensor(gate_c[:, i, :], ada[:, 8 * gate:8 * gate + 8, w], factor,
                                     col("norm_g", 8 * g, 8), ALU.mult, ALU.mult).then_inc(S("mods"), 1)

    def mod_scale(i):
        return lambda k: mod_g[:, i, k:k + 4]

    def mod_shift(i):
        w, _, shift, _ = MODS[i]
        return lambda k: ada[:, 8 * shift + k:8 * shift + k + 4, w]

    def gate_rows_pool(pool, n):
        pool.wait_ge(*S("mods", 9))
        pool.wait_ge(*S("act_lo", 4 * (n_turns(n) + 1)))
        if n == 2:
            pool.wait_ge(*S("hm_lo", 4))
        for h in range(2):
            pool.tensor_tensor(xn[:, 0, 512 * h:512 * h + 512].rearrange("p (a b) -> p a b", a=4), over(ident),
                               per_head(gate_c[:, n, 4 * h:4 * h + 4]), ALU.mult)\
                .then_inc(S("gate_diag"), 1)

    def n_turns(n):
        return (4, 6, 7, 8)[n]

    def gate_rows_pe(pe, n):
        for h in range(2):
            pe.wait_ge(*S("gate_diag", 2 * n + h + 1))
            wait_from(pe, *S("gate_row", 2 * n + h))
            pe.matmul(ps[3][:, :], ones, xn[:, 0, 512 * h:512 * h + 512], start=True, stop=True)\
                .then_inc(S("gate_ps"), 1)

    def gate_rows_act(act, n):
        for h in range(2):
            act.wait_ge(*S("gate_ps", 2 * n + h + 1))
            if n == 0:
                act.wait_ge(*S("ln_done", 8))
            wait_from(act, *S("res_scaled", 4 * n))
            act.copy(gb[:, 0, 512 * h:512 * h + 512], ps[3][:, :]).then_inc(S("gate_row"), 1)

    res_ss = sm(4).rearrange("p (t h) -> p t h", t=2)
    res_rn, rms_ss = sm(2), sm(2)

    def res_act(act, n, y, q):
        act.wait_ge(*S("used", q.first + q.n))
        for tt in range(TT):
            for h in range(2):
                act.activation(xn[:, tt, 512 * h:512 * h + 512], y(tt, h), ACT.Square,
                               accum_out=res_ss[:, tt, h:h + 1]).then_inc(S("res_sq"), 1)

    def res_pool(pool, n, x, w):
        pool.wait_ge(*S("res_sq", 4 * n + 4))
        pool.tensor_tensor(res_rn, res_ss[:, :, 0], res_ss[:, :, 1], ALU.add).then_inc(S("res_a"), 1)
        pool.wait_ge(*S("res_a", 2 * n + 1))
        pool.tensor_scalar(res_rn, res_rn, 1.0 / D, EPS, ALU.mult, ALU.add).then_inc(S("res_a"), 1)
        pool.wait_ge(*S("res_a", 2 * n + 2))
        pool.tensor_tensor(res_rn, res_rn, half_neg[:, 0:2], ALU.pow).then_inc(S("res_rn"), 1)
        for tt in range(TT):
            pool.wait_ge(*S("res_scaled", 4 * n + 2 * tt + 2))
            pool.tensor_tensor(x[:, tt, :], x[:, tt, :], xn[:, tt, :], ALU.add).then_inc(S("res"), 1)

    def res_dve(dve, n, y):
        dve.wait_ge(*S("res_rn", n + 1))
        dve.wait_ge(*S("gate_row", 2 * n + 2))
        for tt in range(TT):
            for h in range(2):
                dve.scalar_tensor_tensor(xn[:, tt, 512 * h:512 * h + 512], y(tt, h),
                                         res_rn[:, tt:tt + 1], gb[:, 0, 512 * h:512 * h + 512],
                                         ALU.mult, ALU.mult).then_inc(S("res_scaled"), 1)

    def rms_act(act, n, x, sem, count, step=1):
        for tt in range(TT):
            act.wait_ge(*S(sem, count + step * tt))
            act.activation(xn[:, tt, :], x[:, tt, :], ACT.Square, accum_out=rms_ss[:, tt:tt + 1])\
               .then_inc(S("rms_sq"), 1)

    def rms_pool(pool, n):
        for tt in range(TT):
            c = rms_ss[:, tt:tt + 1]
            pool.wait_ge(*S("rms_sq", 2 * n + tt + 1))
            pool.tensor_scalar(c, c, 1.0 / D, EPS, ALU.mult, ALU.add).then_inc(S("rms_mean"), 1)
            pool.wait_ge(*S("rms_mean", 2 * n + tt + 1))
            pool.tensor_tensor(c, c, half_neg[:, 0:1], ALU.pow).then_inc(S("rms_rn"), 1)

    def rms_dve(dve, n, x):
        for tt in range(TT):
            dve.wait_ge(*S("rms_rn", 2 * n + tt + 1))
            dve.tensor_scalar(xn[:, tt, :], x[:, tt, :], rms_ss[:, tt:tt + 1], None, ALU.mult)\
               .then_inc(S("rows_ready"), 1)

    def ffn_banks(tt, h):
        return ps[4 + 2 * tt + h][:, :]

    NH, W1 = M_HEADS, MD + 1
    kt = at("kt", 0, [P, KD, T])
    k_tok = at("k_tok", 8, [P, TT, D])
    v_aug = at("v_aug", 16, [P, TT, NH, W1])
    qt = at("qt", 25.125, [P, KD, T])
    hsum = at("hsum", 33.125, [P, TT, NH, MD])
    tap_x = at("tap_x", 41.125, [P, RING, 2 * T])
    tap_y = at("tap_y", 67, [P, RING, 2 * T])
    kw = [at(f"kw{i}", (24.0625, 65.375)[i], [P, MD]) for i in range(2)]
    cell = at("cell", 47.125, [P, 2, NH, 2, W1])
    m_rows = at("m_rows", 41.125, [P, 2, 512])
    m_cm = at("m_cm", 45.125, [P, 2, 256])
    m_a = at("m_a", 67, [P, 2, 256])
    m_em = at("m_em", 69, [P, 2, 256])
    m_wk = at("m_wk", 71, [P, 2, 256])
    m_nq = at("m_nq", 63.25, [P, 2, W1])
    m_gate = sm(32).rearrange("p (t d c h) -> p t d c h", t=2, d=2, c=2)
    m_sp, m_mx = (sm(16).rearrange("p (t d h) -> p t d h", t=2, d=2) for _ in range(2))
    m_state = sm(6).rearrange("p (d n) -> p d n", d=2)
    m_nlast, m_dec = (sm(4).rearrange("p (d n) -> p d n", d=2) for _ in range(2))
    m_dd = sm(16).rearrange("p (d n h) -> p d n h", d=2, n=2)
    m_cols = sm(80)
    m_col = m_cols[:, 0:64].rearrange("p (d t c h) -> p d t c h", d=2, t=2, c=4)
    m_decb = m_cols[:, 64:80].rearrange("p (d n h) -> p d n h", d=2, n=2)
    m_den = sm(4)
    CONVS = {"c_k": 0, "l_k": 1, "l_q": 2}
    IN_COL = {"c_k": 12, "l_k": 12, "l_q": 4}
    TAP_COL = {"c_k": 8, "l_k": 8, "l_q": 0}

    def conv_act(act, name, dst):
        q, n = segs[name], CONVS[name]

        def silu(j):
            act.wait_ge(*S("taps3", 6 * (4 * n + j) + 6))
            slot = (q.first + j) % RING
            act.activation(dst[:, 2 * j:2 * j + 2, :].rearrange("p a t -> p (a t)"),
                           tap_y[:, slot, :], ACT.Silu).then_inc(S("conv3"), 1)
        for j in range(q.n):
            c = q.first + j
            slot = c % RING
            act.wait_ge(*S("used", c + 1))
            wait_from(act, *S("taps3", 6 * (4 * n + j - RING) + 6))
            for f in range(2):
                act.activation(tap_x[:, slot, T * f:T * f + T], ps[slot][:, T * f:T * f + T],
                               ACT.Identity, bias=col("b_in", IN_COL[name] + 2 * j + f))\
                   .then_inc(S("tap_in" if f == 0 else "taken"), 1)
            if j:
                silu(j - 1)
            cut_ahead(act, q, j, slot, c // RING)
        silu(q.n - 1)

    def conv_dve(dve, name):
        q, n = segs[name], CONVS[name]
        for j in range(q.n):
            c = q.first + j
            slot, i0 = c % RING, 6 * (4 * n + j)
            dve.wait_ge(*S("taken", q.before["taken"] + j + 1))
            dve.wait_ge(*S("tap_in", 4 * n + j + 1))
            wait_from(dve, *S("conv3", 4 * n + j - RING + 1))
            k = TAP_COL[name] + 2 * j
            x = [tap_x[:, slot, T * f:T * f + T] for f in range(2)]
            y = [tap_y[:, slot, T * f:T * f + T] for f in range(2)]
            for f in range(2):
                dve.tensor_scalar(y[f], x[f], col("conv_w", 16 + k + f), col("conv_b", k + f),
                                  ALU.mult, ALU.add).then_inc(S("taps3"), 1)
            for f in range(2):
                dve.wait_ge(*S("taps3", i0 + f + 1))
                dve.scalar_tensor_tensor(y[f][:, 1:T], x[f][:, 0:T - 1], col("conv_w", k + f),
                                         y[f][:, 1:T], ALU.mult, ALU.add).then_inc(S("taps3"), 1)
            for f in range(2):
                dve.wait_ge(*S("taps3", i0 + f + 3))
                dve.scalar_tensor_tensor(y[f][:, 0:T - 1], x[f][:, 1:T], col("conv_w", 32 + k + f),
                                         y[f][:, 0:T - 1], ALU.mult, ALU.add).then_inc(S("taps3"), 1)
            cut_ahead(dve, q, j, slot, c // RING)

    def values_dve(dve, name):
        q = segs[name]
        dve.wait_ge(*S("vrow_in", 16))
        for j in range(q.n):
            c = q.first + j
            dve.wait_ge(*S("used", c + 1))
            dve.tensor_tensor(v_aug[:, :, j, 0:MD], bank(c % RING, 2),
                              gb[:, 1, CC * j:CC * j + CC].unsqueeze(1).to_broadcast([P, TT, CC]),
                              ALU.add).then_inc(S("taken"), 1)
            cut_ahead(dve, q, j, c % RING, c // RING)

    def m_gates_dve(dve, n):
        dve.wait_ge(*S("gates_ps", n + 2))
        flat_g = m_gate.rearrange("p t d c h -> p t (d c h)")
        dve.tensor_tensor(flat_g, ps[7][:, 0:32].rearrange("p (t c) -> p t c", t=2),
                          gate_bias.unsqueeze(1).to_broadcast([P, 2, 16]), ALU.add)\
           .then_inc(S("m_gate"), 1)
        dve.wait_ge(*S("m_gate", n + 1))
        f = m_gate[:, :, :, 1, :]
        dve.tensor_scalar(m_mx, f, -1.0, 0.0, ALU.mult, ALU.max).then_inc(S("m_soft"), 1)
        dve.tensor_scalar(m_sp, f, -1.0, None, ALU.mult).then_inc(S("m_soft"), 1)
        dve.wait_ge(*S("m_soft", 4 * n + 2))
        dve.tensor_tensor(m_sp, m_sp, f, ALU.max).then_inc(S("m_soft"), 1)
        dve.wait_ge(*S("m_log", n + 1))
        dve.tensor_tensor(m_sp, m_sp, m_mx, ALU.add).then_inc(S("m_soft"), 1)

    def m_gates_act(act, n):
        act.wait_ge(*S("m_soft", 4 * n + 3))
        act.activation(m_sp, m_sp, ACT.Exp, scale=-1.0).then_inc(S("m_exp"), 1)
        act.wait_ge(*S("m_exp", n + 1))
        act.activation(m_sp, m_sp, ACT.Ln, bias=1.0).then_inc(S("m_log"), 1)

    def tile_of(d, p):
        return p if d == 0 else 1 - p

    def m_rows_pe(pe, n):
        pe.wait_ge(*S("m_soft", 4 * n + 4))
        pe.wait_ge(*S("act_lo", 4 * (6 + 2 * n)))
        for d in range(2):
            u = tab("uf" if d == 0 else "ub")
            for tt in range(TT):
                pe.matmul(ps[4 + d][0:4, tt * P:tt * P + P], m_gate[:, tt, d, 0, :], ident,
                          start=True, stop=False)
                pe.matmul(ps[4 + d][0:4, tt * P:tt * P + P], m_sp[:, tt, d, :], u,
                          start=False, stop=True)
                last = pe.matmul(ps[4 + d][0:4, T + tt * P:T + tt * P + P], m_sp[:, tt, d, :], u,
                                 start=True, stop=True)
            last.then_inc(S("m_rows_ps"), 1)

    def m_rows_dve(dve, n):
        for d in range(2):
            dve.wait_ge(*S("m_rows_ps", 2 * n + d + 1))
            dve.wait_ge(*S("conv3", 4 if n == 0 else 12))
            dve.tensor_copy(m_rows[0:4, d, :], ps[4 + d][0:4, :]).then_inc(S("m_rows"), 1)
        if n == 0:
            dve.memset(m_state[0:4, :, 0:1], 0.0).then_inc(S("m_first"), 1)
        else:
            dve.tensor_copy(m_state[0:4, :, 0:1], m_state[0:4, :, 2:3]).then_inc(S("m_first"), 1)
        dve.wait_ge(*S("m_rows", 2 * n + 2))
        dve.wait_ge(*S("m_first", n + 1))
        for p in range(2):
            for d in range(2):
                at_ = tile_of(d, p) * P
                i = 4 * n + 2 * p + d
                r = m_rows[0:4, d, at_:at_ + P]
                cm = m_cm[0:4, d, at_:at_ + P]
                if d:
                    r, cm = r[:, ::-1], cm[:, ::-1]
                wait_from(dve, *S("m_next", i - 1))
                dve.tensor_tensor_scan(cm, r, r, m_state[0:4, d, p:p + 1], ALU.max, ALU.max)\
                   .then_inc(S("m_scan"), 1)
            for d in range(2):
                at_ = tile_of(d, p) * P + (P - 1 if d == 0 else 0)
                i = 4 * n + 2 * p + d
                dve.wait_ge(*S("m_scan", i + 1))
                last = m_cm[0:4, d, at_:at_ + 1]
                dve.tensor_tensor(m_state[0:4, d, p + 1:p + 2], last, m_rows[0:4, d, T + at_:T + at_ + 1],
                                  ALU.subtract).then_inc(S("m_next"), 1)
                dve.tensor_scalar(m_nlast[0:4, d, p:p + 1], last, -1.0, None, ALU.mult)\
                   .then_inc(S("m_nlast"), 1)
        dve.wait_ge(*S("m_nlast", 4 * n + 4))
        dve.tensor_tensor(m_dec[0:4, :, :], m_state[0:4, :, 0:2], m_nlast[0:4, :, :], ALU.add)\
           .then_inc(S("m_ddiff"), 1)
        if n:
            dve.tensor_tensor(m_em[0:4, :, :], m_cm[0:4, :, :], m_rows[0:4, :, T:2 * T], ALU.subtract)\
               .then_inc(S("m_mt"), 1)
        dve.wait_ge(*S("m_dec", n + 1))
        dve.tensor_tensor(m_dd[0:4, :, :, :].rearrange("p d n h -> p (d n) h"),
                          ident[0:4, 0:4].unsqueeze(1).to_broadcast([4, 4, 4]),
                          m_dec[0:4, :, :].rearrange("p d n -> p (d n)").unsqueeze(2)
                          .to_broadcast([4, 4, 4]), ALU.mult).then_inc(S("m_dd"), 1)
        dve.wait_ge(*S("m_cols_ps", n + 1))
        if n:
            dve.tensor_copy(m_cols, ps[6][:, 0:80]).then_inc(S("m_cols"), 1)
        else:
            dve.tensor_copy(m_cols[:, 64:80], ps[6][:, 64:80]).then_inc(S("m_cols0"), 1)
            src = ps[6][:, 0:64].rearrange("p (d t c h) -> p (d t) c h", d=2, t=2, c=4)
            dst = m_cols[:, 0:64].rearrange("p (d t c h) -> p (d t) c h", d=2, t=2, c=4)
            dve.tensor_copy(dst[:, :, 0:2, :], src[:, :, 0:2, :]).then_inc(S("m_cols"), 1)

    def m_rows_act(act, n):
        act.wait_ge(*S("m_ddiff", n + 1))
        act.activation(m_dec[0:4, :, :], m_dec[0:4, :, :], ACT.Exp).then_inc(S("m_dec"), 1)
        for p in range(2):
            for d in range(2):
                at_ = tile_of(d, p) * P
                c = slice(at_, at_ + P)
                act.activation(m_wk[0:4, d, c], m_rows[0:4, d, c], ACT.Exp,
                               bias=m_nlast[0:4, d, p:p + 1]).then_inc(S("m_wk"), 1)
                if n:
                    act.activation(m_a[0:4, d, c], m_cm[0:4, d, c], ACT.Exp, scale=-1.0,
                                   bias=m_state[0:4, d, p:p + 1]).then_inc(S("m_a"), 1)
        if n:
            act.wait_ge(*S("m_mt", 1))
            act.activation(m_em[0:4, :, :], m_em[0:4, :, :], ACT.Exp, scale=-1.0)\
               .then_inc(S("m_em"), 1)

    def m_cols_pe(pe, n):
        pe.wait_ge(*S("m_wk", 4 * n + 4))
        if n:
            pe.wait_ge(*S("m_a", 4))
            pe.wait_ge(*S("m_em", 1))
        kinds = [m_rows, m_wk] + ([m_a, m_em] if n else [])
        for d in range(2):
            for tt in range(TT):
                for c, row in enumerate(kinds):
                    at_ = ((d * 2 + tt) * 4 + c) * 4
                    pe.matmul(ps[6][:, at_:at_ + 4], row[0:4, d, tt * P:tt * P + P], ident[0:4, 0:4],
                              start=True, stop=True)
        pe.wait_ge(*S("m_dd", n + 1))
        pe.matmul(ps[6][:, 64:80], ones[0:4, :], m_dd[0:4, :, :, :].rearrange("p d n h -> p (d n h)"),
                  start=True, stop=True).then_inc(S("m_cols_ps"), 1)

    def k_tok_pe(pe, n):
        for b in range(4):
            tt, kh = b // 2, b % 2
            pe.wait_ge(*S("conv3", 4 if n == 0 else 8))
            wait_from(pe, *S("k_tok", 4 * n + b - 1 if b > 1 else 0))
            dst = ps[(3, 7)[b % 2]]
            if b < 2:
                pe.wait_ge(*S("m_gate", n + 1))
            for k in range(4):
                last = pe.transpose(dst[:, k * P:k * P + P], kt[:, 4 * kh + k, tt * P:tt * P + P], ident)
            last.then_inc(S("k_tok_ps"), 1)

    def k_tok_act(act, n):
        for b in range(4):
            tt, kh = b // 2, b % 2
            act.wait_ge(*S("k_tok_ps", 4 * n + b + 1))
            if b == 0:
                wait_from(act, *S("cell", 8 * 2 * n))
            act.mul(k_tok[:, tt, 512 * kh:512 * kh + 512], ps[(3, 7)[b % 2]][:, :], MD ** -0.5)\
               .then_inc(S("k_tok"), 1)

    UPDATES = [(0, d, p, h) for p in range(2) for d in range(2) for h in range(NH)] + \
              [(1, d, 0, h) for d in range(2) for h in range(NH)]

    def update_pe(pe, u):
        n, d, p, h = UPDATES[u]
        tt = tile_of(d, p)
        pe.wait_ge(*S("kw", u + 1))
        pe.wait_ge(*S("taken", segs[("c_v", "l_v")[n]].before["taken"] + 4))
        pe.wait_ge(*S("ones_col", 1))
        wait_from(pe, *S("cell", 2 * (u - 1)))
        if u in (0, 16):
            pe.wait_ge(*S("m_cols", n + 1))
        for kk in range(2):
            last = pe.matmul(ps[4 + 2 * (u % 2) + kk][:, 0:W1], kw[u % 2][:, kk * P:kk * P + P],
                             v_aug[:, tt, h, :], start=True, stop=True)
        last.then_inc(S("cell_ps"), 1)

    def update_act(act, u):
        n, d, p, h = UPDATES[u]
        tt = tile_of(d, p)
        act.wait_ge(*S("m_cols", n + 1))
        act.wait_ge(*S("k_tok", 4 * n + 4))
        wait_from(act, *S("cell_ps", u - 1))
        act.activation(kw[u % 2][:, :], k_tok[:, tt, h * MD:h * MD + MD], ACT.Copy,
                       scale=m_col[:, d, tt, 1, h:h + 1]).then_inc(S("kw"), 1)

    def update_dve(dve, u):
        n, d, p, h = UPDATES[u]
        dve.wait_ge(*S("cell_ps", u + 1))
        wait_from(dve, *S("cell", 2 * u - 14))
        for kk in range(2):
            c, b = cell[:, d, h, kk, :], ps[4 + 2 * (u % 2) + kk][:, 0:W1]
            if n == 0 and p == 0:
                ins = dve.tensor_copy(c, b)
            else:
                ins = dve.scalar_tensor_tensor(c, c, m_decb[:, d, p, h:h + 1], b, ALU.mult, ALU.add)
            ins.then_inc(S("cell"), 1)

    PASSES = [(0, 0), (1, 0), (0, 1), (1, 1)]

    def pass_pe(pe, s):
        d, p = PASSES[s]
        tt = tile_of(d, p)
        tile = slice(tt * P, tt * P + P)
        pe.wait_ge(*S("m_cols", 2))
        wait_from(pe, *S("w_diff", s))
        wait_from(pe, *S("s_t", s))
        if s == 0:
            pe.wait_ge(*S("k_tok", 8))
            pe.wait_ge(*S("taken", segs["l_q"].before["taken"] + 4))
            pe.wait_ge(*S("conv3", 12))
        for h in range(NH):
            pe.matmul(bank(3, 4)[:, h, :], tab("sel", 4)[0:4, h, :], m_cm[0:4, d, tile],
                      start=True, stop=True)
        pe.matmul(bank(3, 4)[:, 3, :], tab("sel", 4)[0:4, 3, :], m_cm[0:4, d, tile],
                  start=True, stop=True).then_inc(S("cm_ps"), 1)
        wait_from(pe, *S("hden", 4 * s))
        wait_from(pe, *S("nq", 4 * s))
        for h in range(NH):
            for kk in range(2):
                last = pe.matmul(bank(2, 4)[:, h, :], kt[:, 2 * h + kk, tile], qt[:, 2 * h + kk, tile],
                                 start=(kk == 0), stop=(kk == 1))
        last.then_inc(S("st_ps"), 1)
        pe.wait_ge(*S("cell", 32 if p == 0 else 48))

        def qc(h):
            i = 4 * s + h
            wait_from(pe, *S("nq", i))
            for kk in range(2):
                last = pe.matmul(ps[0][:, 0:W1], qt[:, 2 * h + kk, tile], cell[:, d, h, kk, :],
                                 start=(kk == 0), stop=(kk == 1))
            last.then_inc(S("qc_ps"), 1)

        def sv(h):
            i = 4 * s + h
            wait_from(pe, *S("num", i))
            pe.wait_ge(*S("s_t", s + 1))
            pe.matmul(ps[1][:, 0:W1], s_t(s)[:, h, :], v_aug[:, tt, h, :], start=True, stop=True)\
                .then_inc(S("sv_ps"), 1)
        for h in range(NH):
            qc(h)
            sv(h)
            if p == 0:
                update_pe(pe, 16 + 4 * d + h)

    def s_t(s):
        return tadd[:, s % 2, :].rearrange("p (a b) -> p a b", a=4)

    def pass_act(act, s):
        d, p = PASSES[s]
        tt = tile_of(d, p)
        act.wait_ge(*S("w_pos", s + 1))
        act.activation(s_t(s), s_t(s), ACT.Exp, scale=-1.0).then_inc(S("w_exp"), 1)
        for h in range(NH):
            i = 4 * s + h
            if p == 0:
                update_act(act, 16 + 4 * d + h)
            act.wait_ge(*S("qc_ps", i + 1))
            wait_from(act, *S("hout", i - 1))
            act.activation(m_nq[:, i % 2, :], ps[0][:, 0:W1], ACT.Copy,
                           scale=m_col[:, d, tt, 2, h:h + 1]).then_inc(S("nq"), 1)

    def pass_dve(dve, s):
        d, p = PASSES[s]
        tt = tile_of(d, p)
        dve.wait_ge(*S("cm_ps", s + 1))
        wait_from(dve, *S("sv_ps", 4 * (s - 1)))
        if s < 2:
            dve.wait_ge(*S("gate_ps", 4))
        dve.tensor_tensor(s_t(s), bank(3, 4), per_head(m_col[:, d, tt, 0, :]), ALU.subtract)\
           .then_inc(S("w_diff"), 1)
        dve.wait_ge(*S("w_mask", s + 1))
        dve.wait_ge(*S("st_ps", s + 1))
        dve.scalar_tensor_tensor(s_t(s), bank(2, 4), MD ** -0.5, s_t(s), ALU.mult, ALU.mult)\
           .then_inc(S("s_t"), 1)
        for h in range(NH):
            i = 4 * s + h
            dve.wait_ge(*S("sv_ps", i + 1))
            dve.wait_ge(*S("nq", i + 1))
            nq = m_nq[:, i % 2, :]
            dve.tensor_tensor(nq, nq, ps[1][:, 0:W1], ALU.add).then_inc(S("num"), 1)
            dve.wait_ge(*S("num", i + 1))
            den = m_den[:, i % 2:i % 2 + 1]
            dve.tensor_scalar(den, nq[:, MD:W1], -1.0, m_col[:, d, tt, 3, h:h + 1],
                              ALU.mult, ALU.max).then_inc(S("hneg"), 1)
            dve.wait_ge(*S("hneg", i + 1))
            dve.tensor_tensor(den, den, nq[:, MD:W1], ALU.max).then_inc(S("hden"), 1)
            dve.wait_ge(*S("hden", i + 1))
            dve.reciprocal(den, den).then_inc(S("hrec"), 1)
            dve.wait_ge(*S("hrec", i + 1))
            out_h = hsum[:, tt, h, :]
            if s < 2:
                ins = dve.tensor_scalar(out_h, nq[:, 0:MD], den, None, ALU.mult)
            else:
                dve.wait_ge(*S("hout", 8))
                ins = dve.scalar_tensor_tensor(out_h, nq[:, 0:MD], den, out_h, ALU.mult, ALU.add)
            ins.then_inc(S("hout"), 1)
            if p == 0:
                update_dve(dve, 16 + 4 * d + h)

    def pass_pool(pool, s):
        d, _ = PASSES[s]
        pool.wait_ge(*S("w_diff", s + 1))
        pool.tensor_scalar(s_t(s), s_t(s), 0.0, None, ALU.max).then_inc(S("w_pos"), 1)
        pool.wait_ge(*S("w_exp", s + 1))
        pool.tensor_tensor(s_t(s), s_t(s), over(tab("uf" if d == 0 else "ub")), ALU.mult)\
            .then_inc(S("w_mask"), 1)

    xft = at("xft", 68, [P, 4, T])
    sig_o = at("sig_o", 25.125, [P, KD, T])
    sig_b = at("sig_b", 48, [P, 16, T])
    tokt = at("tokt", 41.125, [P, 2, TT, T])
    zf = at("zf", 72, [P, TT, 2, 2 * P])
    yfh, yfl = at("yfh", 16, [P, 4, T], F32R), at("yfl", 20, [P, 4, T], F32R)
    hmh, hml = at("hmh", 0, [P, KD, T], F32R), at("hml", 8, [P, KD, T], F32R)
    hsq = at("hsq", 0, [P, TT, NH, MD])
    y_four = at("y_four", 33.125, [P, KD, T])
    y_mix = at("y_mix", 0, [P, TT, D])
    h_rn = sm(8)

    def lat_in_act(act):
        for name, dst, func, b0 in (("l_f", xft, ACT.Identity, ("b_in", 0)),
                                    ("l_o", sig_o, ACT.Sigmoid, ("b_in", 28)),
                                    ("l_br", sig_b, ACT.Sigmoid, ("b_br", 0))):
            q = segs[name]
            for j in range(q.n):
                c = q.first + j
                act.wait_ge(*S("used", c + 1))
                if name == "l_f" and j == 0:
                    act.wait_ge(*S("hout", 16))
                for f in range(2):
                    act.activation(dst[:, 2 * j + f, :], ps[c % RING][:, T * f:T * f + T], func,
                                   bias=col(b0[0], b0[1] + 2 * j + f))\
                       .then_inc(S("sig_first" if f == 0 else "taken"), 1)
                cut_ahead(act, q, j, c % RING, c // RING)

    def head_norm_pool(pool):
        pool.wait_ge(*S("hout", 16))
        pool.tensor_tensor(hsq[:, :, :, :].rearrange("p a b c -> p (a b c)"),
                           hsum[:, :, :, :].rearrange("p a b c -> p (a b c)"),
                           hsum[:, :, :, :].rearrange("p a b c -> p (a b c)"), ALU.mult)\
            .then_inc(S("hsq"), 1)
        pool.wait_ge(*S("hss", 1))
        pool.tensor_scalar(h_rn, h_rn, 1.0 / MD, EPS, ALU.mult, ALU.add).then_inc(S("hmean"), 1)
        pool.wait_ge(*S("hmean", 1))
        pool.tensor_tensor(h_rn, h_rn, half_neg[:, 0:8], ALU.pow).then_inc(S("h_rn"), 1)
        pool.wait_ge(*S("taken", segs["l_o"].before["taken"] + 4))
        pool.tensor_tensor(sig_o[:, :, :], sig_o[:, :, :],
                           col("head_g", 0, 8).unsqueeze(2).to_broadcast([P, 8, T]), ALU.mult)\
            .then_inc(S("sig_og"), 1)

    def head_norm_dve(dve):
        v = hsum[:, :, :, :].rearrange("p a b c -> p (a b) c")
        dve.wait_ge(*S("hsq", 1))
        dve.tensor_reduce(h_rn, hsq[:, :, :, :].rearrange("p a b c -> p (a b) c"), AX, ALU.add)\
           .then_inc(S("hss"), 1)
        dve.wait_ge(*S("h_rn", 1))
        dve.tensor_tensor(v, v, h_rn.unsqueeze(2).to_broadcast([P, 8, MD]), ALU.mult)\
           .then_inc(S("hnorm"), 1)

    def merge_pe(pe):
        pe.wait_ge(*S("tok_in", 16))
        pe.wait_ge(*S("taken", segs["l_br"].before["taken"] + 8))
        for half in range(2):
            for tt in range(TT):
                if half:
                    pe.wait_ge(*S("zf", 2))
                for g in range(2):
                    x = xft[:, 2 * half + g, tt * P:tt * P + P]
                    for cs, name in enumerate(("cd", "nsd")):
                        last = pe.matmul(ps[tt][:, cs * T + g * P:cs * T + g * P + P], x, tab(name),
                                         start=True, stop=True)
                last.then_inc(S("zf_ps"), 1)
            pe.wait_ge(*S("zf", 2 * half + 2))
            if half:
                pe.wait_ge(*S("yf_lo", 1))
            for g in range(2):
                o = ps[2][:, g * T:g * T + T]
                for i, (cs, tt) in enumerate([(0, 0), (0, 1), (1, 0), (1, 1)]):
                    last = pe.matmul(o, zf[:, tt, cs, g * P:g * P + P], tokt[:, cs, tt, :],
                                     start=(i == 0), stop=(i == 3))
            last.then_inc(S("yf_ps"), 1)
        for b in range(4):
            tt, kh = b // 2, b % 2
            pe.wait_ge(*S("hnorm", 1))
            for k in range(4):
                f = 4 * kh + k
                last = pe.transpose(ps[4 + b][:, k * P:k * P + P],
                                    hsum[:, tt, f // 2, (f % 2) * P:(f % 2) * P + P], ident)
            last.then_inc(S("hm_ps"), 1)
        pe.wait_ge(*S("yf_lo", 2))
        stream_pe(pe, "four", yfh, yfl)
        pe.wait_ge(*S("hm_lo", 4))
        stream_pe(pe, "mproj", hmh, hml)
        pe.wait_ge(*S("y_lo", 4))
        stream_pe(pe, "w_out", ah, al)

    def merge_act(act):
        for half in range(2):
            for tt in range(TT):
                act.wait_ge(*S("zf_ps", 2 * half + tt + 1))
                wait_from(act, *S("yf_ps", half))
                act.copy(zf[:, tt, :, :].rearrange("p a b -> p (a b)"), ps[tt][:, :])\
                   .then_inc(S("zf"), 1)
            act.wait_ge(*S("yf_ps", half + 1))
            act.copy(yfh[:, 2 * half:2 * half + 2, :], bank(2, 2)).then_inc(S("yf"), 1)
        for b in range(4):
            act.wait_ge(*S("hm", b + 1))
            act.copy(feat(hmh, b), hm_tmp(b)).then_inc(S("hm_hi"), 1)
        skip_cuts(act, "four")
        q = segs["mproj"]
        for j in range(q.n):
            c = q.first + j
            act.wait_ge(*S("y_sum", j + 1))
            act.copy(ah[:, 2 * j:2 * j + 2, :], sig_b[:, 8 + 2 * j:10 + 2 * j, :])\
               .then_inc(S("y_hi"), 1)
            cut_ahead(act, q, j, c % RING, c // RING)
        q = segs["w_out"]
        for j in range(q.n):
            c = q.first + j
            act.wait_ge(*S("used", c + 1))
            act.copy(y_mix[:, :, CC * j:CC * j + CC], bank(c % RING, 2)).then_inc(S("taken"), 1)
            cut_ahead(act, q, j, c % RING, c // RING)

    def hm_tmp(b):
        return zf[:, :, :, :].rearrange("p a b c -> p (a b c)")[:, (b % 2) * 512:(b % 2) * 512 + 512]\
            .rearrange("p (a b) -> p a b", a=4)

    def merge_dve(dve):
        for half in range(2):
            dve.wait_ge(*S("yf", half + 1))
            dve.tensor_tensor(yfl[:, 2 * half:2 * half + 2, :], bank(2, 2),
                              yfh[:, 2 * half:2 * half + 2, :].bitcast(F32), ALU.subtract)\
               .then_inc(S("yf_lo"), 1)
        dve.wait_ge(*S("yf_ps", 2))
        dve.wait_ge(*S("sig_og", 1))

        def lo(b):
            dve.wait_ge(*S("hm_hi", b + 1))
            dve.tensor_tensor(feat(hml, b), hm_tmp(b), feat(hmh, b).bitcast(F32), ALU.subtract)\
               .then_inc(S("hm_lo"), 1)
        for b in range(4):
            if b >= 2:
                lo(b - 2)
                dve.wait_ge(*S("hm_lo", b - 1))
            dve.wait_ge(*S("hm_ps", b + 1))
            dve.tensor_tensor(hm_tmp(b), bank(4 + b, 4), feat(sig_o, b), ALU.mult)\
               .then_inc(S("hm"), 1)
        lo(2)
        lo(3)
        q = segs["four"]
        for j in range(q.n):
            c = q.first + j
            dve.wait_ge(*S("used", c + 1))
            dve.tensor_tensor(y_four[:, 2 * j:2 * j + 2, :], bank(c % RING, 2),
                              sig_b[:, 2 * j:2 * j + 2, :], ALU.mult).then_inc(S("taken"), 1)
            cut_ahead(dve, q, j, c % RING, c // RING)
        q = segs["mproj"]
        for j in range(q.n):
            c = q.first + j
            y = sig_b[:, 8 + 2 * j:10 + 2 * j, :]
            dve.wait_ge(*S("used", c + 1))
            dve.tensor_tensor(y, bank(c % RING, 2), y, ALU.mult).then_inc(S("taken"), 1)
            dve.wait_ge(*S("taken", q.before["taken"] + j + 1))
            dve.tensor_tensor(y, y, y_four[:, 2 * j:2 * j + 2, :], ALU.add).then_inc(S("y_sum"), 1)
            cut_ahead(dve, q, j, c % RING, c // RING)
            dve.wait_ge(*S("y_hi", j + 1))
            dve.tensor_tensor(al[:, 2 * j:2 * j + 2, :], y, ah[:, 2 * j:2 * j + 2, :].bitcast(F32),
                              ALU.subtract).then_inc(S("y_lo"), 1)
        q = segs["w_out"]
        walk(dve, q, lambda j, slot, turn: cut_ahead(dve, q, j, slot, turn))

    block = ctx.enter_context(nc.Block())

    def scale_of(name, i):
        return lambda k: col(name, i + k, 4)

    def free_at(name):
        return segs[name].first

    def skip_cuts(eng, name):
        q = segs[name]
        walk(eng, q, lambda j, slot, turn: cut_ahead(eng, q, j, slot, turn))

    def mix_rows(tt, h):
        return y_mix[:, tt, 512 * h:512 * h + 512]

    @block.sync
    def _(sp):
        load_stream(sp)

    @block.tensor
    def _(pe):
        params_pe(pe)
        turn_pe(pe, 0, x0)
        gdn_in_pe(pe)
        gdn_prep_pe(pe)
        for tt in range(TT):
            gdn_tokens_pe(pe, tt)
        pe.wait_ge(*S("g_lo", 4))
        stream_pe(pe, "g_out", ah, al)
        turn_pe(pe, 1, xn)
        pe.wait_ge(*S("act_lo", 8))
        ffn_pe(pe, 0)
        turn_pe(pe, 2, xn)
        att_in_pe(pe)
        att_pe(pe)
        pe.wait_ge(*S("o_lo", 8))
        stream_pe(pe, "m_out", ah, al)
        turn_pe(pe, 3, xn)
        pe.wait_ge(*S("act_lo", 16))
        ffn_pe(pe, 1)
        ada_pe(pe)
        turn_pe(pe, 4, xn)
        pe.wait_ge(*S("act_lo", 20))
        ffn_pe(pe, 2, 0)
        turn_pe(pe, 5, xn)
        pe.wait_ge(*S("act_lo", 24))
        gates_pe(pe, 1, 7)
        stream_pe(pe, "c_k", ah, al)
        stream_pe(pe, "c_v", ah, al)
        k_tok_pe(pe, 0)
        m_rows_pe(pe, 0)
        m_cols_pe(pe, 0)
        for u in range(16):
            update_pe(pe, u)
        turn_pe(pe, 6, xn)
        pe.wait_ge(*S("act_lo", 28))
        ffn_pe(pe, 3, 1)
        turn_pe(pe, 7, xn)
        pe.wait_ge(*S("act_lo", 32))
        gates_pe(pe, 2, 7)
        for name in ("l_k", "l_v", "l_q"):
            stream_pe(pe, name, ah, al)
        k_tok_pe(pe, 1)
        m_rows_pe(pe, 1)
        m_cols_pe(pe, 1)
        for s in range(4):
            pass_pe(pe, s)
        pe.wait_ge(*S("w_diff", 4))
        pe.wait_ge(*S("nq", 16))
        pe.wait_ge(*S("num", 16))
        for name in ("l_f", "l_o", "l_br"):
            stream_pe(pe, name, ah, al)
        merge_pe(pe)
        gate_rows_pe(pe, 2)
        turn_pe(pe, 8, xn)
        pe.wait_ge(*S("act_lo", 36))
        ffn_pe(pe, 4, 3)

    @block.scalar
    def _(act):
        load_params(act)
        small_weight_load(act, 0, A["a_w_in"][0], 4096)
        start_cuts(act)
        params_act(act)
        turn_act(act, 0, 0)
        gdn_in_act(act)
        gdn_prep_act(act)
        for tt in range(TT):
            gdn_tokens_act(act, tt)
        ln_rows_load(act, 0, A["ln1_g"][0:1], A["ln1_b"][0:1])
        skip_cuts(act, "g_out")
        turn_act(act, 1, segs["g_out"].first + 4)
        ffn_act(act, 0)
        ln_rows_load(act, 1, A["ln2_g"][0:1], A["ln2_b"][0:1])
        turn_act(act, 2, segs["down0"].first)
        att_in_act(act)
        att_act(act)
        ln_rows_load(act, 2, A["ln1_g"][1:2], A["ln1_b"][1:2])
        skip_cuts(act, "m_out")
        turn_act(act, 3, segs["m_out"].first + 4)
        ffn_act(act, 1)
        ln_rows_load(act, 3, A["ln2_g"][1:2], A["ln2_b"][1:2])
        ada_act(act)
        act.wait_ge(*S("ln_done", 8))
        act.dma_start(gb[:, 1, :], A["b_in_2"][:, COL_V:COL_V + D].broadcast_to([P, D]))\
           .then_inc(S("vrow_in"), 16)
        small_weight_load(act, 1, w_in, COL_GATES)
        rms_act(act, 0, x1, "ctx_in", 16, 0)
        turn_act(act, 4, segs["up2"].first)
        ffn_act(act, 2, 0)
        res_act(act, 0, ffn_banks, segs["down2"])
        rms_act(act, 1, x1, "res", 1)
        turn_act(act, 5, segs["c_k"].first)
        m_gates_act(act, 0)
        conv_act(act, "c_k", kt)
        skip_cuts(act, "c_v")
        k_tok_act(act, 0)
        m_rows_act(act, 0)
        for u in range(16):
            update_act(act, u)
        rms_act(act, 2, x0, "cell_ps", 16, 0)
        turn_act(act, 6, segs["up3"].first)
        ffn_act(act, 3, 1)
        res_act(act, 1, ffn_banks, segs["down3"])
        rms_act(act, 3, x0, "res", 3)
        turn_act(act, 7, segs["l_k"].first)
        m_gates_act(act, 1)
        conv_act(act, "l_k", kt)
        skip_cuts(act, "l_v")
        conv_act(act, "l_q", qt)
        k_tok_act(act, 1)
        m_rows_act(act, 1)
        for s in range(4):
            pass_act(act, s)
        act.wait_ge(*S("hout", 16))
        act.dma_start(tokt[:, :, :, :].rearrange("p a b c -> p (a b c)"), A["tok"])\
           .then_inc(S("tok_in"), 16)
        lat_in_act(act)
        merge_act(act)
        gate_rows_act(act, 2)
        act.wait_ge(*S("taken", segs["w_out"].before["taken"] + 4))
        res_act(act, 2, mix_rows, segs["w_out"])
        rms_act(act, 4, x0, "res", 5)
        turn_act(act, 8, segs["up4"].first)
        ffn_act(act, 4, 3)
        res_act(act, 3, ffn_banks, segs["down4"])
        for tt in range(TT):
            act.wait_ge(*S("res", 7 + tt))
            act.dma_start(out[tt * P:tt * P + P, :], x0[:, tt, :]).then_inc(S("out_done"), 16)
        act.wait_ge(*S("out_done", 32))

    @block.vector
    def _(dve):
        start_cuts(dve)
        turn_dve(dve, 0)
        gdn_in_dve(dve)
        gdn_prep_dve(dve)
        for tt in range(TT):
            gdn_tokens_dve(dve, tt)
        ln_sums_of_chunks(dve, 0, segs["g_out"])
        ln_rows(dve, 0)
        turn_dve(dve, 1, scale_of("ln1_g", 0))
        ffn_dve(dve, 0)
        ln_sums_of_banks(dve, 1, segs["down0"])
        ln_rows(dve, 1)
        turn_dve(dve, 2, scale_of("ln2_g", 0))
        att_in_dve(dve)
        att_dve(dve)
        ln_sums_of_chunks(dve, 2, segs["m_out"])
        ln_rows(dve, 2)
        turn_dve(dve, 3, scale_of("ln1_g", 8))
        ffn_dve(dve, 1)
        ln_sums_of_banks(dve, 3, segs["down1"])
        ln_rows(dve, 3, "ln_last")
        ada_dve(dve)
        small_weight_cut(dve, 1)
        rms_dve(dve, 0, x1)
        turn_dve(dve, 4, mod_scale(0))
        ffn_dve(dve, 2)
        res_dve(dve, 0, ffn_banks)
        rms_dve(dve, 1, x1)
        turn_dve(dve, 5, mod_scale(1))
        m_gates_dve(dve, 0)
        conv_dve(dve, "c_k")
        values_dve(dve, "c_v")
        m_rows_dve(dve, 0)
        for u in range(16):
            update_dve(dve, u)
        rms_dve(dve, 2, x0)
        turn_dve(dve, 6, mod_scale(2))
        ffn_dve(dve, 3)
        res_dve(dve, 1, ffn_banks)
        rms_dve(dve, 3, x0)
        turn_dve(dve, 7, mod_scale(3))
        m_gates_dve(dve, 1)
        conv_dve(dve, "l_k")
        values_dve(dve, "l_v")
        conv_dve(dve, "l_q")
        m_rows_dve(dve, 1)
        for s in range(4):
            pass_dve(dve, s)
        head_norm_dve(dve)
        for name in ("l_f", "l_o", "l_br"):
            skip_cuts(dve, name)
        merge_dve(dve)
        res_dve(dve, 2, mix_rows)
        rms_dve(dve, 4, x0)
        turn_dve(dve, 8, mod_scale(4))
        ffn_dve(dve, 4)
        res_dve(dve, 3, ffn_banks)

    @block.gpsimd
    def _(pool):
        setup_pool(pool)
        gdn_in_pool(pool)
        gdn_prep_pool(pool)
        for tt in range(TT):
            gdn_tokens_pool(pool, tt)
        ln_pool(pool, 0)
        turn_pool(pool, 1, scale_of("ln1_b", 0))
        ln_affine_pool(pool, 0, "rows_ready", 0)
        ln_pool(pool, 1)
        turn_pool(pool, 2, scale_of("ln2_b", 0))
        ln_affine_pool(pool, 1, "rows_ready", 2)
        ln_pool(pool, 2)
        turn_pool(pool, 3, scale_of("ln1_b", 8))
        ln_affine_pool(pool, 2, "rows_ready", 4)
        ln_pool(pool, 3)
        ln_affine_pool(pool, 3, "ln_last", 0)
        ada_pool(pool)
        rms_pool(pool, 0)
        turn_pool(pool, 4, mod_shift(0))
        gate_rows_pool(pool, 0)
        res_pool(pool, 0, x1, 0)
        rms_pool(pool, 1)
        turn_pool(pool, 5, mod_shift(1))
        pool.memset(v_aug[:, :, :, MD:W1], 1.0).then_inc(S("ones_col"), 1)
        rms_pool(pool, 2)
        turn_pool(pool, 6, mod_shift(2))
        gate_rows_pool(pool, 1)
        res_pool(pool, 1, x0, 0)
        rms_pool(pool, 3)
        turn_pool(pool, 7, mod_shift(3))
        pool.memset(v_aug[:, :, :, MD:W1], 1.0).then_inc(S("ones_col"), 1)
        for s in range(4):
            pass_pool(pool, s)
        head_norm_pool(pool)
        gate_rows_pool(pool, 2)
        res_pool(pool, 2, x0, 0)
        rms_pool(pool, 4)
        turn_pool(pool, 8, mod_shift(4))
        gate_rows_pool(pool, 3)
        res_pool(pool, 3, x0, 0)
    ctx.close()


def kernel(**inputs):
    import concourse.bacc as bacc
    from concourse.bass_utils import run_bass_kernel_spmd

    table, tok = shape_tables()
    arrays = {name: np.ascontiguousarray(v) for name, v in inputs.items() if np.asarray(v).size}
    arrays["table"], arrays["tok"] = table, tok
    nc = bacc.Bacc("TRN2", target_bir_lowering=False, num_devices=1)
    A = {name: nc.dram_tensor("in_" + name, v.shape, F32, kind="ExternalInput").ap()
         for name, v in arrays.items()}
    out = nc.dram_tensor("out", [T, D], F32, kind="ExternalOutput").ap()
    build(nc, A, out)
    r = run_bass_kernel_spmd(nc, [{"in_" + name: v for name, v in arrays.items()}], core_ids=[0])
    return r.results[0]["out"].reshape(1, T, D)
```
